# Optimizing a Trainium2 kernel written in Bass

```python
import jax, jax.numpy as jnp
from jax import lax
import numpy as np

D_MODEL = 2048
BATCH = 1
SEQ = 256
DEPTH = 1

ATT_HEADS = 16
ATT_KV_HEADS = 2
ATT_HEAD_DIM = 64
ATT_WIDTH = ATT_HEADS * ATT_HEAD_DIM
ATT_KV_WIDTH = ATT_KV_HEADS * ATT_HEAD_DIM
WINDOW = 128
ATT_BLOCK = 128
ROPE_DIM = ATT_HEAD_DIM // 4
ROPE_THETA = 500000.0
M_HEADS = 4
M_QK_DIM = 128
M_V_DIM = 256
M_QK_WIDTH = M_HEADS * M_QK_DIM
M_WIDTH = M_HEADS * M_V_DIM
M_CHUNK = 64
CONV_WIDTH = 4
D_FF = 5632
NORM_EPS = 1e-6
NEG_INF = -1e30
N_MOD = 9
PROJ_SIZES = (ATT_WIDTH, ATT_KV_WIDTH, ATT_KV_WIDTH,
              2 * M_QK_WIDTH, M_WIDTH,
              M_HEADS, M_HEADS, M_WIDTH,
              2 * D_MODEL)
PROJ_OUT = sum(PROJ_SIZES)

kernel_name = "hybrid_swa_mlstm_macaron_adaln"

def _split_cols(t, sizes):
    idx = np.cumsum(sizes)[:-1].tolist()
    return jnp.split(t, idx, axis=-1)

def _rmsnorm(x, g):
    x32 = x.astype(jnp.float32)
    y = x32 * lax.rsqrt(jnp.mean(x32 * x32, axis=-1, keepdims=True) + NORM_EPS)
    return y.astype(x.dtype) * g

def _modulate(x, shift, scale):
    return x * (1 + scale) + shift

def _swiglu(x, w_in, w_out):
    a, b = jnp.split(x @ w_in, 2, axis=-1)
    return (jax.nn.silu(a) * b) @ w_out

def _partial_rope(x, positions):
    half = ROPE_DIM // 2
    inv_freq = jnp.power(ROPE_THETA, -jnp.arange(half, dtype=jnp.float32) * 2.0 / ROPE_DIM)
    ang = positions.astype(jnp.float32)[..., None] * inv_freq
    cos, sin = jnp.cos(ang)[:, :, None, :], jnp.sin(ang)[:, :, None, :]
    xr = x[..., :ROPE_DIM].astype(jnp.float32)
    x1, x2 = xr[..., :half], xr[..., half:]
    rot = jnp.concatenate([x1 * cos - x2 * sin, x2 * cos + x1 * sin], axis=-1)
    return jnp.concatenate([rot.astype(x.dtype), x[..., ROPE_DIM:]], axis=-1)

def _sliding_window_attention(q, k, v, sinks):
    B, T, Hq, hd = q.shape
    nb = T // ATT_BLOCK
    G = Hq // ATT_KV_HEADS
    qb = q.reshape(B, nb, ATT_BLOCK, ATT_KV_HEADS, G, hd)

    def band(t):
        tp = jnp.pad(t, ((0, 0), (ATT_BLOCK, 0), (0, 0), (0, 0)))
        prev = tp[:, :T].reshape(B, nb, ATT_BLOCK, ATT_KV_HEADS, hd)
        cur = t.reshape(B, nb, ATT_BLOCK, ATT_KV_HEADS, hd)
        return jnp.concatenate([prev, cur], axis=2)

    kb, vb = band(k), band(v)
    s = jnp.einsum('bnqhgd,bnkhd->bnhgqk', qb, kb,
                   preferred_element_type=jnp.float32) * (hd ** -0.5)
    qi = jnp.arange(ATT_BLOCK)[:, None] + ATT_BLOCK
    kj = jnp.arange(2 * ATT_BLOCK)[None, :]
    band_ok = (kj <= qi) & (kj > qi - WINDOW)
    blk_ok = (jnp.arange(nb)[:, None, None] > 0) | (kj[None] >= ATT_BLOCK)
    mask = band_ok[None] & blk_ok
    s = jnp.where(mask[None, :, None, None], s, NEG_INF)
    sink = sinks.astype(jnp.float32).reshape(1, 1, ATT_KV_HEADS, G, 1, 1)
    m = jnp.maximum(jnp.max(s, axis=-1, keepdims=True), sink)
    p = jnp.exp(s - m)
    denom = jnp.sum(p, axis=-1, keepdims=True) + jnp.exp(sink - m)
    o = jnp.einsum('bnhgqk,bnkhd->bnqhgd', (p / denom).astype(v.dtype), vb)
    return o.reshape(B, T, Hq * hd)

def _causal_conv(x, w, b):
    C = x.shape[-1]
    y = lax.conv_general_dilated(x, w[:, None, :].astype(x.dtype), window_strides=(1,),
                                 padding=((CONV_WIDTH - 1, 0),),
                                 dimension_numbers=('NWC', 'WIO', 'NWC'),
                                 feature_group_count=C)
    return y + b

def _mlstm_chunkwise(q, k, v, i_pre, f_pre):
    B, T, H, dk = q.shape
    dv = v.shape[-1]
    L = M_CHUNK
    nc = T // L
    f32 = jnp.float32

    def chunks(t):
        return jnp.moveaxis(t.astype(f32).reshape(B, nc, L, H, -1), 3, 1)

    qc = chunks(q)
    kc = chunks(k) * (dk ** -0.5)
    vc = chunks(v)
    ig = jnp.moveaxis(i_pre.astype(f32).reshape(B, nc, L, H), 3, 1)
    logf = jax.nn.log_sigmoid(jnp.moveaxis(f_pre.astype(f32).reshape(B, nc, L, H), 3, 1))
    bcum = jnp.cumsum(logf, axis=-1)
    b_last = bcum[..., -1]
    g = b_last[..., None] - bcum + ig
    g_max = jnp.max(g, axis=-1)
    w = jnp.exp(g - g_max[..., None])
    C_loc = jnp.einsum('bhcl,bhcld,bhcle->bhcde', w, kc, vc)
    n_loc = jnp.einsum('bhcl,bhcld->bhcd', w, kc)

    def step(carry, inp):
        C, n, m = carry
        Cl, nl, gm, bl = inp
        m_new = jnp.maximum(bl + m, gm)
        a = jnp.exp(bl + m - m_new)
        s = jnp.exp(gm - m_new)
        C_new = a[..., None, None] * C + s[..., None, None] * Cl
        n_new = a[..., None] * n + s[..., None] * nl
        return (C_new, n_new, m_new), (C, n, m)

    init = (jnp.zeros((B, H, dk, dv), f32), jnp.zeros((B, H, dk), f32),
            jnp.full((B, H), NEG_INF, f32))
    xs = (jnp.moveaxis(C_loc, 2, 0), jnp.moveaxis(n_loc, 2, 0),
          jnp.moveaxis(g_max, 2, 0), jnp.moveaxis(b_last, 2, 0))
    _, (C_in, n_in, m_in) = lax.scan(step, init, xs)
    C_in = jnp.moveaxis(C_in, 0, 2)
    n_in = jnp.moveaxis(n_in, 0, 2)
    m_in = jnp.moveaxis(m_in, 0, 2)

    a_log = bcum + m_in[..., None]
    D = bcum[..., :, None] - bcum[..., None, :] + ig[..., None, :]
    causal = jnp.tril(jnp.ones((L, L), dtype=bool))
    D = jnp.where(causal, D, NEG_INF)
    m_t = jnp.maximum(a_log, jnp.max(D, axis=-1))
    inter = jnp.exp(a_log - m_t)
    qk = jnp.einsum('bhctd,bhcsd->bhcts', qc, kc) * jnp.exp(D - m_t[..., None])
    num = (inter[..., None] * jnp.einsum('bhctd,bhcde->bhcte', qc, C_in)
           + jnp.einsum('bhcts,bhcse->bhcte', qk, vc))
    den = inter * jnp.einsum('bhctd,bhcd->bhct', qc, n_in) + jnp.sum(qk, axis=-1)
    h = num / jnp.maximum(jnp.abs(den), jnp.exp(-m_t))[..., None]
    return jnp.moveaxis(h, 1, 3).reshape(B, T, H * dv).astype(v.dtype)

def _head_rmsnorm(h, g):
    B, T, _ = h.shape
    return _rmsnorm(h.reshape(B, T, M_HEADS, M_V_DIM), 1).reshape(B, T, M_WIDTH) * g

def _hybrid_mixer(u, positions, w_in, conv_w, conv_b, b_igate, b_fgate, sinks,
                  mlstm_norm_g, w_att_up, w_mlstm_up, w_out):
    B, T, _ = u.shape
    proj = u @ w_in
    aq, ak, av, mqk, mv, mi, mf, mo, gates = _split_cols(proj, PROJ_SIZES)
    q = _partial_rope(aq.reshape(B, T, ATT_HEADS, ATT_HEAD_DIM), positions)
    k = _partial_rope(ak.reshape(B, T, ATT_KV_HEADS, ATT_HEAD_DIM), positions)
    v = av.reshape(B, T, ATT_KV_HEADS, ATT_HEAD_DIM)
    y_att = _sliding_window_attention(q, k, v, sinks) @ w_att_up
    mqk = jax.nn.silu(_causal_conv(mqk, conv_w, conv_b))
    mq, mk = jnp.split(mqk, 2, axis=-1)
    hm = _mlstm_chunkwise(mq.reshape(B, T, M_HEADS, M_QK_DIM),
                          mk.reshape(B, T, M_HEADS, M_QK_DIM),
                          mv.reshape(B, T, M_HEADS, M_V_DIM),
                          mi + b_igate, mf + b_fgate)
    hm = _head_rmsnorm(hm, mlstm_norm_g) * jax.nn.sigmoid(mo)
    y_m = hm @ w_mlstm_up
    g_att, g_m = jnp.split(jax.nn.sigmoid(gates), 2, axis=-1)
    return (g_att * y_att + g_m * y_m) @ w_out

def setup_inputs(seed: int = 0) -> dict:
    key = jax.random.key(seed)
    ks = jax.random.split(key, 24)
    f32 = jnp.float32
    D = D_MODEL

    def nrm(k, shape, scale):
        return jax.random.normal(k, shape, f32) * scale

    x = nrm(ks[0], (BATCH, SEQ, D), 1.0)
    c = nrm(ks[1], (BATCH, D), 1.0)
    offset = jax.random.randint(ks[2], (BATCH, 1), 0, 4096, dtype=jnp.int32)
    positions = (offset + jnp.arange(SEQ, dtype=jnp.int32)[None, :]).astype(jnp.int32)
    return {
        'x': x,
        'c': c,
        'positions': positions,
        'w_ada': nrm(ks[3], (DEPTH, D, N_MOD * D), 0.5 * D ** -0.5),
        'b_ada': nrm(ks[4], (DEPTH, N_MOD * D), 0.02),
        'norm1_g': 1.0 + nrm(ks[5], (DEPTH, D), 0.02),
        'ffn1_w_in': nrm(ks[6], (DEPTH, D, 2 * D_FF), D ** -0.5),
        'ffn1_w_out': nrm(ks[7], (DEPTH, D_FF, D), D_FF ** -0.5),
        'norm2_g': 1.0 + nrm(ks[8], (DEPTH, D), 0.02),
        'w_in': nrm(ks[9], (DEPTH, D, PROJ_OUT), D ** -0.5),
        'conv_w': nrm(ks[10], (DEPTH, CONV_WIDTH, 2 * M_QK_WIDTH), CONV_WIDTH ** -0.5),
        'conv_b': nrm(ks[11], (DEPTH, 2 * M_QK_WIDTH), 0.02),
        'b_igate': nrm(ks[12], (DEPTH, M_HEADS), 0.1),
        'b_fgate': jnp.linspace(3.0, 6.0, M_HEADS, dtype=f32)[None, :] + nrm(ks[13], (DEPTH, M_HEADS), 0.1),
        'sinks': nrm(ks[14], (DEPTH, ATT_HEADS), 1.0),
        'mlstm_norm_g': 1.0 + nrm(ks[15], (DEPTH, M_WIDTH), 0.02),
        'w_att_up': nrm(ks[16], (DEPTH, ATT_WIDTH, D), ATT_WIDTH ** -0.5),
        'w_mlstm_up': nrm(ks[17], (DEPTH, M_WIDTH, D), M_WIDTH ** -0.5),
        'w_out': nrm(ks[18], (DEPTH, D, D), D ** -0.5),
        'norm3_g': 1.0 + nrm(ks[19], (DEPTH, D), 0.02),
        'ffn2_w_in': nrm(ks[20], (DEPTH, D, 2 * D_FF), D ** -0.5),
        'ffn2_w_out': nrm(ks[21], (DEPTH, D_FF, D), D_FF ** -0.5),
        'final_g': 1.0 + nrm(ks[22], (D,), 0.02),
    }

def reference(x, c, positions, w_ada, b_ada, norm1_g, ffn1_w_in, ffn1_w_out, norm2_g,
              w_in, conv_w, conv_b, b_igate, b_fgate, sinks, mlstm_norm_g, w_att_up,
              w_mlstm_up, w_out, norm3_g, ffn2_w_in, ffn2_w_out, final_g):
    h = x
    cond = jax.nn.silu(c)
    for l in range(DEPTH):
        mod = cond @ w_ada[l] + b_ada[l]
        sh1, sc1, gt1, sh2, sc2, gt2, sh3, sc3, gt3 = [m[:, None, :] for m in jnp.split(mod, N_MOD, axis=-1)]
        u = _modulate(_rmsnorm(h, norm1_g[l]), sh1, sc1)
        h = h + 0.5 * gt1 * _swiglu(u, ffn1_w_in[l], ffn1_w_out[l])
        u = _modulate(_rmsnorm(h, norm2_g[l]), sh2, sc2)
        h = h + gt2 * _hybrid_mixer(u, positions, w_in[l], conv_w[l], conv_b[l], b_igate[l],
                                    b_fgate[l], sinks[l], mlstm_norm_g[l], w_att_up[l],
                                    w_mlstm_up[l], w_out[l])
        u = _modulate(_rmsnorm(h, norm3_g[l]), sh3, sc3)
        h = h + 0.5 * gt3 * _swiglu(u, ffn2_w_in[l], ffn2_w_out[l])
    return _rmsnorm(h, final_g)


_drawn_inputs = setup_inputs


def setup_inputs(seed=0):
    import zlib

    import numpy as np

    out = dict(_drawn_inputs(seed))
    spreads = {}
    factors = {'b_ada': 3.692,
     'norm1_g': 8.0,
     'norm2_g': 8.0,
     'conv_b': 200.0,
     'b_igate': 200.0,
     'sinks': 64.0,
     'mlstm_norm_g': 173.365,
     'norm3_g': 24.266,
     'final_g': 22.374,
     'conv_w': 4.383}
    for name, (base, spread) in spreads.items():
        noise = np.random.default_rng([zlib.crc32(name.encode()), seed]).standard_normal(out[name].shape)
        drawn = base * np.exp(spread * noise) if base else spread * noise
        out[name] = __import__('jax').numpy.asarray(drawn.astype(out[name].dtype))
    for name, factor in factors.items():
        out[name] = (out[name] * factor).astype(out[name].dtype)
    return out
```

```python
from contextlib import ExitStack

import numpy as np
import concourse.bass as bass
from concourse import mybir

F32 = mybir.dt.float32
F32R = mybir.dt.float32r
I32 = mybir.dt.int32
ALU = mybir.AluOpType
ACT = mybir.ActivationFunctionType
AX = mybir.AxisListType

P = 128
NC = 512
RING = 4
ADA_RING = 4
ADA_W = 1024
EPS = 1e-6
NEG = -1e30
ROPE_THETA = 500000.0
WINDOW = 128
TWO_PI_A = 6.28125
TWO_PI_B = float(np.float32(np.floor((2 * np.pi - 6.28125) * 2 ** 20) / 2 ** 20))
TWO_PI_C = float(2 * np.pi - 6.28125 - TWO_PI_B)
ROUND_MAGIC = 12582912.0


class Phase:

    def __init__(self, n, per, c0, a0, b0, nat0):
        self.n, self.per, self.c0, self.a0, self.b0, self.nat0 = n, per, c0, a0, b0, nat0


def build(nc, x, c, positions, w_ada, b_ada, norm1_g, ffn1_w_in, ffn1_w_out, norm2_g, w_in,
          conv_w, conv_b, b_igate, b_fgate, sinks, mlstm_norm_g, w_att_up, w_mlstm_up, w_out,
          norm3_g, ffn2_w_in, ffn2_w_out, final_g, out):
    T, D = x.shape[1], x.shape[2]
    TT = T // P
    KD = D // P
    FF = ffn1_w_out.shape[1]
    HQ = sinks.shape[1]
    ATT = w_att_up.shape[1]
    HD = ATT // HQ
    MH = b_igate.shape[1]
    MW = w_mlstm_up.shape[1]
    MV = MW // MH
    MQK2 = conv_w.shape[2]
    DK = MQK2 // (2 * MH)
    CONV = conv_w.shape[1]
    KVW = (w_in.shape[2] - ATT - MQK2 - 2 * MW - 2 * MH - 2 * D) // 2
    KV = KVW // HD
    OK = ATT
    OV = OK + KVW
    OM = OV + KVW
    OMV = OM + MQK2
    OI = OMV + MW
    OF = OI + MH
    OO = OF + MH
    OG = OO + MW
    ROT = HD // 4
    HALF = ROT // 2
    assert TT == 2 and KD == 16 and DK == P and WINDOW == P and MV == 2 * P and KV == 2

    PARTS = (4, 4, 3)
    assert sum(PARTS) * NC == FF
    plan = {}
    total = [0, 0, 0, 0]

    def plan_phase(name, iters, chunks, a, b, nat=0):
        plan[name] = Phase(iters, chunks, *total)
        for k, more in enumerate((iters * chunks, a, b, nat)):
            total[k] += more

    def plan_ffn(f):
        for p, g in enumerate(PARTS):
            plan_phase(f"ffn{f}_in{p}", g, 8, g, 0, g)
            plan_phase(f"ffn{f}_out{p}", 4, 4, 2, 2)

    plan_ffn(1)
    plan_phase("proj", 4, 8, 4, 4)
    plan_phase("rest", 1, 4, 1, 0)
    plan_phase("gates", 4, 8, 4, 4)
    plan_phase("up", 4, 4, 4, 4, 4)
    plan_phase("wout", 4, 4, 2, 2)
    plan_ffn(2)
    REST_W = OG - 8 * NC
    ada_plan = {"start0": (0, 0, 32), "start1": (1, 0, 32), "ffn1_in0": (2, 0, 32),
                "ffn1_in1": (3, 0, 32), "ffn1_out1": (4, 0, 16), "ffn1_out2": (4, 8, 16),
                "proj": (5, 0, 32), "gates": (6, 0, 32), "up": (7, 0, 16), "wout": (7, 8, 16),
                "ffn2_in0": (8, 0, 32)}
    ada_first = {}
    ada_end = {}
    t = 0
    for name, (m, k0, n) in ada_plan.items():
        ada_first[name] = t
        t += n
        ada_end[m] = t
    SH1, SC1, GT1, SH2, SC2, GT2, SH3, SC3, GT3 = range(9)

    with ExitStack() as ctx:
        def sb(name, shape, dt=F32):
            return ctx.enter_context(nc.sbuf_tensor(name, shape, dt))

        def psum(name, shape):
            return ctx.enter_context(nc.psum_tensor(name, shape, F32))

        def sem(name):
            return ctx.enter_context(nc.semaphore(name))

        h = sb("h", [P, TT, D])
        with nc.sbuf_tensor("raw", [P, RING, 4, NC], F32) as raw:
            pass
        lo = sb("lo", [P, RING, 4, NC], F32R)
        hi = sb("hi", [P, RING, 2, NC], F32R)
        scratch = {}
        with ExitStack() as inner:
            def tmp(name, shape, dt=F32):
                scratch[name] = inner.enter_context(nc.sbuf_tensor(name, shape, dt))
                return scratch[name]
            s_sb = tmp("s_sb", [P, 2, 3 * P])
            p_t = tmp("p_t", [P, 2, 3, P])
            q_st = tmp("q_st", [P, TT, 2 * HD])
            q_t = tmp("q_t", [HD, 2, T])
            k_t = tmp("k_t", [HD, KV, T])
            m_st = tmp("m_st", [P, 16, 4])
            r_row = tmp("r_row", [P, MH, T])
            xpad = tmp("xpad", [P, 2, CONV - 1 + T])
            mq_t = tmp("mq_t", [P, 2, T])
            w_sb = tmp("w_sb", [P, 3 * P])
            a_sb = tmp("a_sb", [P, 3 * P])
            a_t = tmp("a_t", [P, 3, P])
            hm = tmp("hm", [P, TT, MV])
            rope_t = tmp("rope_t", [P, 4, (HQ + KV) * HALF])
        act_hi = sb("act_hi", [P, KD, T], F32R)
        act_lo = sb("act_lo", [P, KD, T], F32R)
        ada_w = sb("ada_w", [P, ADA_RING, ADA_W])
        ada_acc = sb("ada_acc", [P, 2, ADA_W])
        buf_a = sb("buf_a", [P, TT, NC])
        buf_b = sb("buf_b", [P, TT, NC])
        ident = sb("ident", [P, P])
        ones = sb("ones", [P, P])
        tri = sb("tri", [P, P])
        mask = sb("mask", [P, 2 * P])
        dg = sb("dg", [P, 4, P])
        par_in = sb("par_in", [P, P])
        par = sb("par", [P, P])
        bada_in = sb("bada_in", [P, 2, P])
        bada = sb("bada", [P, 9 * KD])
        cond = sb("cond", [P, KD])
        mod = sb("mod", [P, 9, KD])
        gain = sb("gain", [P, KD])
        st = sb("st", [P, 8, 2])
        sink_row = sb("sink_row", [P, HQ])
        gb_row = sb("gb_row", [P, 2, MH])
        inv_f = sb("inv_f", [P, HALF])
        pos_i = sb("pos_i", [P, TT], I32)
        ang = sb("ang", [P, 8, TT, HALF])
        with ExitStack() as inner:
            hid_hi = inner.enter_context(nc.sbuf_tensor("hid_hi", [P, KD, T], F32R))
            hid_lo = inner.enter_context(nc.sbuf_tensor("hid_lo", [P, KD, T], F32R))
            pad = inner.enter_context(nc.sbuf_tensor("pad", [P, 1024], F32))
            gt_row = inner.enter_context(nc.sbuf_tensor("gt_row", [P, D], F32))
            fin_row = inner.enter_context(nc.sbuf_tensor("fin_row", [P, D], F32))
        proj = sb("proj", [P, TT, OG])
        gates = sb("gates", [P, TT, 2 * D])

        pa = psum("pa", [P, TT, NC])
        pb = psum("pb", [P, TT, NC])
        px = psum("px", [P, 2, NC])
        pm = psum("pm", [P, NC])
        pr = psum("pr", [P, NC])

        params_in = sem("params_in")
        rows_in = sem("rows_in")
        x_in = sem("x_in")
        fin_in = sem("fin_in")
        raw_in = [sem(f"raw_in{r}") for r in range(RING)]
        ada_in = [sem(f"ada_in{r}") for r in range(ADA_RING)]
        consts = sem("consts")
        par_tr = sem("par_tr")
        par_ok = sem("par_ok")
        cond_ok = sem("cond_ok")
        hi_done = sem("hi_done")
        lo_done = sem("lo_done")
        unit_used = sem("unit_used")
        ada_done = sem("ada_done")
        flushed = sem("flushed")
        mod_ok = sem("mod_ok")
        pa_free = sem("pa_free")
        pb_free = sem("pb_free")
        silu_ok = sem("silu_ok")
        nat_ok = sem("nat_ok")
        nat_tr = sem("nat_tr")
        nat_hi = sem("nat_hi")
        nat_lo = sem("nat_lo")
        gt_diag = sem("gt_diag")
        gt_mm = sem("gt_mm")
        gt_ok = sem("gt_ok")
        out_tmp = sem("out_tmp")
        h_ok = sem("h_ok")
        ss_ok = sem("ss_ok")
        rt_ok = sem("rt_ok")
        diag_ok = sem("diag_ok")
        xt_mm = sem("xt_mm")
        xt_f = sem("xt_f")
        xt_hi = sem("xt_hi")
        xt_lo = sem("xt_lo")
        dve_step = sem("dve_step")
        act_step = sem("act_step")
        up_part = sem("up_part")
        proj_ok = sem("proj_ok")
        rope_ang = sem("rope_ang")
        trig_ok = sem("trig_ok")
        rope_ok = sem("rope_ok")
        kt_mm = sem("kt_mm")
        kt_ok = sem("kt_ok")
        q_in = sem("q_in")
        q_mm = sem("q_mm")
        q_ok = sem("q_ok")
        sc_mm = sem("sc_mm")
        mx_ok = sem("mx_ok")
        p_ok = sem("p_ok")
        pt_mm = sem("pt_mm")
        pt_ok = sem("pt_ok")
        o_mm = sem("o_mm")
        o_ok = sem("o_ok")
        g_abs = sem("g_abs")
        g_ln = sem("g_ln")
        g_logf = sem("g_logf")
        g_cum = sem("g_cum")
        g_diag = sem("g_diag")
        g_row = sem("g_row")
        g_rowok = sem("g_rowok")
        m_tr = sem("m_tr")
        m_pad = sem("m_pad")
        m_conv = sem("m_conv")
        m_qk = sem("m_qk")
        m_sc = sem("m_sc")
        m_max = sem("m_max")
        m_w = sem("m_w")
        m_a = sem("m_a")
        m_at = sem("m_at")
        m_atok = sem("m_atok")
        m_num = sem("m_num")
        m_h = sem("m_h")
        m_ss = sem("m_ss")
        m_var = sem("m_var")
        m_rt = sem("m_rt")
        m_out = sem("m_out")
        mo_ok = sem("mo_ok")
        fin_ok = sem("fin_ok")
        stored = sem("stored")

        PAR = {}
        par_rows = []
        for name, src, n in (("g1", norm1_g.rearrange("a (k p) -> (a k) p", p=P), KD),
                             ("g2", norm2_g.rearrange("a (k p) -> (a k) p", p=P), KD),
                             ("g3", norm3_g.rearrange("a (k p) -> (a k) p", p=P), KD),
                             ("conv_w", conv_w.rearrange("a j (k p) -> (a j k) p", p=P), CONV * MQK2 // P),
                             ("conv_b", conv_b.rearrange("a (k p) -> (a k) p", p=P), MQK2 // P),
                             ("c", c.rearrange("a (k p) -> (a k) p", p=P), KD),
                             ("mg", mlstm_norm_g.rearrange("a (k p) -> (a k) p", p=P), MW // P)):
            PAR[name] = len(par_rows) and sum(r[1] for r in par_rows)
            par_rows.append((src, n, PAR[name]))
        NPAR = sum(r[1] for r in par_rows)
        assert NPAR <= P
        bada_rows = b_ada.rearrange("a (k p) -> (a k) p", p=P)
        NB = 9 * KD
        x_tok = x.rearrange("a (t p) d -> (a p) t d", p=P)
        out_tok = out.rearrange("a (t p) d -> (a p) t d", p=P)
        wada = w_ada.rearrange("a (k p) n -> p (a k) n", p=P)
        w_ffn_in = {1: ffn1_w_in.rearrange("a (k p) n -> p (a k) n", p=P),
                    2: ffn2_w_in.rearrange("a (k p) n -> p (a k) n", p=P)}
        w_ffn_out = {1: ffn1_w_out.rearrange("a (k p) n -> p (a k) n", p=P),
                     2: ffn2_w_out.rearrange("a (k p) n -> p (a k) n", p=P)}
        w_in_k = w_in.rearrange("a (k p) n -> p (a k) n", p=P)
        w_att_k = w_att_up.rearrange("a (k p) n -> p (a k) n", p=P)
        w_m_k = w_mlstm_up.rearrange("a (k p) n -> p (a k) n", p=P)
        w_out_k = w_out.rearrange("a (k p) n -> p (a k) n", p=P)

        def over(eng, n, body):
            body(0, True)
            if n > 1:
                with eng.Fori(1, n) as i:
                    body(i, False)

        block = ctx.enter_context(nc.Block())

        @block.sync
        def _(sp):
            off = 0
            for src, n, row in par_rows:
                sp.dma_start(par_in[row:row + n, :], src).then_inc(params_in, 16)
            sp.dma_start(bada_in[:, 0, :], bada_rows[0:P, :]).then_inc(params_in, 16)
            sp.dma_start(bada_in[0:NB - P, 1, :], bada_rows[P:NB, :]).then_inc(params_in, 16)

            def load_ada(name, i, j):
                m, k0, n = ada_plan[name]
                per = plan[name].per if name in plan else 8
                tile = ada_first[name] + per * i + j
                if not (isinstance(tile, int) and tile < ADA_RING):
                    sp.wait_ge(ada_done, tile - (ADA_RING - 1))
                kt = k0 + (per // 2) * i + j // 2
                sp.dma_start(ada_w[:, j % ADA_RING, :],
                             wada[:, bass.ds(kt, 1), m * D + (j % 2) * ADA_W:m * D + (j % 2 + 1) * ADA_W])\
                    .then_inc(ada_in[j % ADA_RING], 16)

            def load(ph, i, j, src, kn, w=NC):
                cidx = ph.c0 + ph.per * i + j
                if not (isinstance(cidx, int) and cidx < RING):
                    sp.wait_ge(unit_used, 2 * (cidx - (RING - 1)))
                sp.dma_start(raw[:, j % RING, 0:kn, 0:w], src).then_inc(raw_in[j % RING], 16)

            for name in ("start0", "start1"):
                def start(i, first, name=name):
                    for j in range(8):
                        load_ada(name, i, j)
                over(sp, 4, start)
                if name == "start0":
                    sp.dma_start(h[:, :, :], x_tok).then_inc(x_in, 16)
                    sp.dma_start(pos_i[:, :], positions.rearrange("a (t p) -> (a p) t", p=P),
                                 allow_slow_non_contiguous=True).then_inc(rows_in, 16)
                    sp.dma_start(sink_row[:, :], sinks.broadcast_to([P, HQ])).then_inc(rows_in, 16)
                    sp.dma_start(gb_row[:, 0, :], b_igate.broadcast_to([P, MH])).then_inc(rows_in, 16)
                    sp.dma_start(gb_row[:, 1, :], b_fgate.broadcast_to([P, MH])).then_inc(rows_in, 16)

            def load_ffn(f):
                g0 = 0
                for p, ng in enumerate(PARTS):
                    name = f"ffn{f}_in{p}"
                    def ffn_in(i, first, name=name, g0=g0):
                        for j in range(8):
                            src = w_ffn_in[f][:, (j % 4) * 4:(j % 4) * 4 + 4,
                                              bass.ds((i + g0) * NC + (j // 4) * FF, NC)]
                            load(plan[name], i, j, src, 4)
                            if name in ada_plan:
                                load_ada(name, i, j)
                    over(sp, ng, ffn_in)
                    name = f"ffn{f}_out{p}"
                    def ffn_out(b, first, name=name, g0=g0, ng=ng):
                        for j in range(4):
                            src = w_ffn_out[f][:, g0 * 4 + j * ng:g0 * 4 + (j + 1) * ng, bass.ds(b * NC, NC)]
                            load(plan[name], b, j, src, ng)
                            if name in ada_plan:
                                load_ada(name, b, j)
                    over(sp, 4, ffn_out)
                    g0 += ng

            load_ffn(1)

            def proj_pair(name, col0):
                def body(i, first):
                    for j in range(8):
                        src = w_in_k[:, (j % 4) * 4:(j % 4) * 4 + 4,
                                     bass.ds(i * (2 * NC) + (col0 + (j // 4) * NC), NC)]
                        load(plan[name], i, j, src, 4)
                        load_ada(name, i, j)
                over(sp, 4, body)

            proj_pair("proj", 0)
            for j in range(4):
                load(plan["rest"], 0, j, w_in_k[:, j * 4:j * 4 + 4, 8 * NC:OG], 4, REST_W)
            proj_pair("gates", OG)

            def up(i, first):
                for j in range(4):
                    w = w_att_k if j < 2 else w_m_k
                    load(plan["up"], i, j, w[:, (j % 2) * 4:(j % 2) * 4 + 4, bass.ds(i * NC, NC)], 4)
                    load_ada("up", i, j)
            over(sp, 4, up)

            def wout(i, first):
                for j in range(4):
                    load(plan["wout"], i, j, w_out_k[:, j * 4:j * 4 + 4, bass.ds(i * NC, NC)], 4)
                    load_ada("wout", i, j)
            over(sp, 4, wout)
            sp.wait_ge(nat_ok, plan["up"].nat0 + 4)
            sp.dma_start(fin_row[:, :], final_g.rearrange("(a d) -> a d", a=1).broadcast_to([P, D]))\
                .then_inc(fin_in, 16)
            load_ffn(2)
            sp.wait_ge(fin_ok, 1)
            sp.dma_start(out_tok[:, 0, :], h[:, 0, :]).then_inc(stored, 16)
            sp.wait_ge(fin_ok, 2)
            sp.dma_start(out_tok[:, 1, :], h[:, 1, :]).then_inc(stored, 16)
            sp.wait_ge(stored, 32)

        @block.gpsimd
        def _(pool):
            pool.memset(ident[:, :], 0.0)
            pool.memset(ones[:, :], 1.0)
            pool.memset(tri[:, :], 1.0)
            pool.memset(mask[:, :], 0.0).then_inc(consts, 1)
            pool.wait_ge(consts, 1)
            pool.affine_select(out=ident[:, :], in_=ident[:, :], compare_op=ALU.not_equal, fill=1.0,
                               base=0, pattern=[[-1, P]], channel_multiplier=1)
            pool.affine_select(out=tri[:, :], in_=tri[:, :], compare_op=ALU.is_ge, fill=0.0,
                               base=0, pattern=[[1, P]], channel_multiplier=-1)
            pool.affine_select(out=mask[:, P:2 * P], in_=mask[:, P:2 * P], compare_op=ALU.is_ge, fill=NEG,
                               base=0, pattern=[[-1, P]], channel_multiplier=1)
            pool.affine_select(out=mask[:, 0:P], in_=mask[:, 0:P], compare_op=ALU.is_ge, fill=NEG,
                               base=-1, pattern=[[1, P]], channel_multiplier=-1).then_inc(consts, 1)

        def units(chunks, kn):
            for j in range(chunks):
                for half in (0, 1):
                    n = min(2, kn - 2 * half)
                    yield j, half, j * kn + 2 * half, n

        @block.tensor
        def _(pe):
            def unit(ph, i, j, half, k0, n, a_hi, a_lo, bank, start, stop, w=NC):
                u = 2 * (ph.c0 + ph.per * i + j) + half
                pe.wait_ge(lo_done, u + 1)
                for kk in range(n):
                    w_hi = hi[:, (2 * j + half) % 4, kk, 0:w]
                    w_lo = lo[:, j % RING, 2 * half + kk, 0:w]
                    for tt in range(TT):
                        tok = slice(tt * P, (tt + 1) * P)
                        ps = bank[:, tt, 0:w]
                        pe.matmul(ps, a_hi[:, k0 + kk, tok], w_hi, start=start and kk == 0, stop=False)
                        pe.matmul(ps, a_hi[:, k0 + kk, tok], w_lo, start=False, stop=False)
                        mm = pe.matmul(ps, a_lo[:, k0 + kk, tok], w_hi, start=False,
                                       stop=stop and kk == n - 1)
                mm.then_inc(unit_used, 1)

            def transposes(nb):
                pe.wait_ge(nat_ok, nb + 1)
                for b in (0, 1):
                    for ft in (0, 1):
                        for tt in range(TT):
                            mm = pe.transpose(px[:, b, ft * T + tt * P:ft * T + (tt + 1) * P],
                                              buf_b[:, tt, (2 * b + ft) * P:(2 * b + ft + 1) * P], ident[:, :])
                    mm.then_inc(nat_tr, 1)

            def flush(m):
                pe.wait_ge(ada_done, ada_end[m])
                if m > 0:
                    pe.wait_ge(mod_ok, m)
                if m > GT1:
                    pe.wait_ge(gt_ok, 4 if m <= GT2 + 2 else 8)
                for s in range(KD):
                    mm = pe.matmul(pm[:, s:s + 1], ada_acc[:, s // 8, (s % 8) * P:(s % 8 + 1) * P],
                                   ones[:, 0:1], start=True, stop=True)
                mm.then_inc(flushed, 1)

            def gate_rows(n):
                pe.wait_ge(gt_diag, n + 1)
                for q in range(4):
                    if q >= 2:
                        pe.wait_ge(gt_ok, 4 * n + q - 1)
                    pe.matmul((pr, pm)[q % 2][:, :], ones[:, :], gt_row[:, q * NC:(q + 1) * NC],
                              start=True, stop=True).then_inc(gt_mm, 1)

            def in_body(ph, i, first, a_hi, a_lo, nat, mid=None):
                if not (isinstance(i, int) and i + ph.a0 == 0):
                    pe.wait_ge(pa_free, ph.a0 + i)
                for j, half, k0, n in units(4, 4):
                    unit(ph, i, j, half, k0, n, a_hi, a_lo, pa, (j, half) == (0, 0), (j, half) == (3, 1))
                    if first and mid and (j, half) == (1, 1):
                        mid()
                if nat and not first:
                    transposes(ph.nat0 + i - 1)
                if nat:
                    if first and ph.b0 > 0:
                        pe.wait_ge(pb_free, ph.b0)
                else:
                    pe.wait_ge(pb_free, ph.b0 + i)
                for j, half, k0, n in units(4, 4):
                    unit(ph, i, 4 + j, half, k0, n, a_hi, a_lo, pb, (j, half) == (0, 0), (j, half) == (3, 1))

            def out_phase(ph, kn, nat_last, flush_m=None, gate=None):
                if flush_m is not None:
                    flush(flush_m)
                for b in range(4):
                    bank, free, use0 = (pa, pa_free, ph.a0) if b % 2 == 0 else (pb, pb_free, ph.b0)
                    if b == 1 and gate is not None:
                        gate_rows(gate)
                    pe.wait_ge(free, use0 + b // 2)
                    for j, half, k0, n in units(4, kn):
                        if b == 0 and k0 < 4 * (kn - 1) < k0 + n + 1 or (b == 0 and k0 == 4 * (kn - 1)):
                            pe.wait_ge(nat_lo, 2 * (nat_last + 1))
                        unit(ph, b, j, half, k0, n, hid_hi, hid_lo, bank, (j, half) == (0, 0),
                             k0 + n == 4 * kn)
                        if b == 0 and (j, half) == (1, 1):
                            transposes(nat_last)

            def turn(rhs0, src, kt0, kts, g0):
                for g in range(kts // 2):
                    if g0 + g >= 2:
                        pe.wait_ge(xt_f, g0 + g - 1)
                    for k in (0, 1):
                        for tt in range(TT):
                            dst = px[:, g % 2, k * T + tt * P:k * T + (tt + 1) * P]
                            s = src(tt, kt0 + 2 * g + k)
                            if rhs0 is None:
                                mm = pe.transpose(dst, s, ident[:, :])
                            else:
                                mm = pe.matmul(dst, s, rhs0(tt), start=True, stop=True)
                    mm.then_inc(xt_mm, 1)

            def norm_turn(n):
                pe.wait_ge(diag_ok, n + 1)
                turn(lambda tt: dg[:, tt, :], lambda tt, k: h[:, tt, k * P:(k + 1) * P], 0, KD,
                     (0, 8, 24)[n])
                pe.wait_ge(xt_lo, (8, 16, 32)[n])

            def ffn(f):
                for p, ng in enumerate(PARTS):
                    ph = plan[f"ffn{f}_in{p}"]
                    over(pe, ng, lambda i, first: in_body(ph, i, first, act_hi, act_lo, True))
                    name = f"ffn{f}_out{p}"
                    out_phase(plan[name], ng, ph.nat0 + ng - 1,
                              flush_m={"ffn1_out0": GT1, "ffn1_out1": SH2, "ffn2_out0": GT3}.get(name),
                              gate={"ffn1_out0": 0, "ffn2_out0": 2}.get(name))

            pe.wait_ge(consts, 2)
            pe.wait_ge(params_in, 16 * (len(par_rows) + 2))
            pe.transpose(px[:, 0, 0:NPAR], par_in[0:NPAR, :], ident[0:NPAR, 0:NPAR])
            pe.transpose(px[:, 0, P:2 * P], bada_in[:, 0, :], ident[:, :])
            pe.transpose(px[:, 0, 2 * P:P + NB], bada_in[0:NB - P, 1, :], ident[0:NB - P, 0:NB - P])\
                .then_inc(par_tr, 1)
            pe.wait_ge(par_ok, 2)
            flush(SH1)
            flush(SC1)
            norm_turn(0)
            ffn(1)
            flush(SC2)
            norm_turn(1)
            over(pe, 4, lambda i, first: in_body(plan["proj"], i, first, act_hi, act_lo, False))
            ph = plan["rest"]
            pe.wait_ge(pa_free, ph.a0)
            for j, half, k0, n in units(4, 4):
                unit(ph, 0, j, half, k0, n, act_hi, act_lo, pa, (j, half) == (0, 0), (j, half) == (3, 1), REST_W)
                if (j, half) == (1, 1):
                    flush(GT2)
            over(pe, 4, lambda i, first: in_body(plan["gates"], i, first, act_hi, act_lo, False))
            flush(SH3)

            pe.wait_ge(rope_ok, 1)
            for g in range(KV):
                for tt in range(TT):
                    mm = pe.transpose(px[0:HD, 0, g * T + tt * P:g * T + (tt + 1) * P],
                                      proj[:, tt, OK + g * HD:OK + (g + 1) * HD], ident[:, :])
            mm.then_inc(kt_mm, 1)
            pe.wait_ge(kt_ok, 1)

            def pair(g, n):
                pe.wait_ge(q_in, n + 1)
                for tt in range(TT):
                    mm = pe.transpose(px[:, 0, tt * P:(tt + 1) * P], q_st[:, tt, :], ident[:, :])
                mm.then_inc(q_mm, 1)
                pe.wait_ge(q_ok, n + 1)
                for hh in (0, 1):
                    pe.matmul(pa[:, 0, hh * P:(hh + 1) * P], q_t[:, hh, 0:P], k_t[:, g, 0:P],
                              start=True, stop=True)
                    mm = pe.matmul(pa[:, 1, hh * T:(hh + 1) * T], q_t[:, hh, P:T], k_t[:, g, :],
                                   start=True, stop=True)
                mm.then_inc(sc_mm, 1)
                pe.wait_ge(p_ok, n + 1)
                for hh in (0, 1):
                    for b in range(3):
                        mm = pe.transpose(pb[:, hh, b * P:(b + 1) * P], s_sb[:, hh, b * P:(b + 1) * P],
                                          ident[:, :])
                mm.then_inc(pt_mm, 1)
                pe.wait_ge(pt_ok, n + 1)
                vs = slice(OV + g * HD, OV + (g + 1) * HD)
                for hh in (0, 1):
                    pe.matmul(px[:, 1, hh * HD:(hh + 1) * HD], p_t[:, hh, 0, :], proj[:, 0, vs],
                              start=True, stop=True)
                    dst = px[:, 1, (2 + hh) * HD:(3 + hh) * HD]
                    pe.matmul(dst, p_t[:, hh, 1, :], proj[:, 0, vs], start=True, stop=False)
                    mm = pe.matmul(dst, p_t[:, hh, 2, :], proj[:, 1, vs], start=False, stop=True)
                mm.then_inc(o_mm, 1)

            NPAIR = HQ // KV // 2
            for g in range(KV):
                with pe.Fori(0, NPAIR) as i:
                    pair(g, i + g * NPAIR)

            pe.wait_ge(g_logf, 1)
            pe.matmul(pm[:, 0:MH], tri[:, :], m_st[:, 0, :], start=True, stop=True)
            pe.matmul(pm[:, MH:2 * MH], tri[:, :], m_st[:, 1, :], start=True, stop=False)
            pe.matmul(pm[:, MH:2 * MH], ones[:, :], m_st[:, 0, :], start=False, stop=True).then_inc(g_cum, 1)
            for tt in range(TT):
                pe.wait_ge(g_diag, tt + 1)
                pe.matmul(pr[:, :] if tt == 0 else pm[:, :], ones[:, :], dg[:, :, :].rearrange("p a b -> p (a b)"),
                          start=True, stop=True).then_inc(g_row, 1)
            pe.wait_ge(o_ok, 2 * NPAIR)
            for hd in range(MH):
                for qk in (0, 1):
                    for tt in range(TT):
                        cs = OM + qk * (MQK2 // 2) + hd * DK
                        mm = pe.transpose(px[:, 0, qk * T + tt * P:qk * T + (tt + 1) * P],
                                          proj[:, tt, cs:cs + DK], ident[:, :])
                mm.then_inc(m_tr, 1)
                pe.wait_ge(m_qk, hd + 1)
                pe.matmul(pa[:, 0, 0:P], mq_t[:, 0, 0:P], mq_t[:, 1, 0:P], start=True, stop=True)
                pe.matmul(pa[:, 0, P:3 * P], mq_t[:, 0, P:T], mq_t[:, 1, :], start=True, stop=True)\
                    .then_inc(m_sc, 1)
                pe.wait_ge(m_a, hd + 1)
                for b in range(3):
                    mm = pe.transpose(pb[:, 0, b * P:(b + 1) * P], a_sb[:, b * P:(b + 1) * P], ident[:, :])
                mm.then_inc(m_at, 1)
                pe.wait_ge(m_atok, hd + 1)
                vs = slice(OMV + hd * MV, OMV + (hd + 1) * MV)
                pe.matmul(px[:, 1, 0:MV], a_t[:, 0, :], proj[:, 0, vs], start=True, stop=True)
                pe.matmul(px[:, 1, MV:2 * MV], a_t[:, 1, :], proj[:, 0, vs], start=True, stop=False)
                pe.matmul(px[:, 1, MV:2 * MV], a_t[:, 2, :], proj[:, 1, vs], start=False, stop=True)\
                    .then_inc(m_num, 1)
            pe.wait_ge(m_out, MH)
            turn(None, lambda tt, k: proj[:, tt, k * P:(k + 1) * P], 0, ATT // P, 16)
            turn(None, lambda tt, k: proj[:, tt, OMV + k * P:OMV + (k + 1) * P], 0, MW // P, 20)
            pe.wait_ge(xt_lo, 24)

            ph = plan["up"]

            def up(i, first):
                pe.wait_ge(pa_free, ph.a0 + i)
                for j, half, k0, n in units(2, 4):
                    unit(ph, i, j, half, k0, n, act_hi, act_lo, pa, (j, half) == (0, 0), (j, half) == (1, 1))
                if not first:
                    transposes(ph.nat0 + i - 1)
                pe.wait_ge(pb_free, ph.b0 + i)
                for j, half, k0, n in units(2, 4):
                    unit(ph, i, 2 + j, half, 8 + k0, n, act_hi, act_lo, pb, (j, half) == (0, 0), (j, half) == (1, 1))
            over(pe, 4, up)
            out_phase(plan["wout"], 4, ph.nat0 + 3, gate=1)
            flush(SC3)
            norm_turn(2)
            ffn(2)

        @block.scalar
        def _(act):
            steps = [0]

            def link(ins):
                steps[0] += 1
                ins.then_inc(act_step, 1)
                act.wait_ge(act_step, steps[0])

            def split(ph, i, j, half, n, w=NC):
                u = 2 * (ph.c0 + ph.per * i + j) + half
                if half == 0:
                    act.wait_ge(raw_in[j % RING], 16 * (ph.c0 // RING + (ph.per // RING) * i + j // RING + 1))
                if not (isinstance(u, int) and u < 4):
                    act.wait_ge(unit_used, u - 3)
                act.copy(hi[:, (2 * j + half) % 4, 0:n, 0:w], raw[:, j % RING, 2 * half:2 * half + n, 0:w])\
                    .then_inc(hi_done, 1)

            def nat_evac_at(nb, slot):
                for b in (0, 1):
                    act.wait_ge(consts, 2)
                    act.wait_ge(nat_tr, 2 * nb + b + 1)
                    k = 4 * slot + 2 * b
                    act.copy(hid_hi[:, bass.ds(k, 2), :], px[:, b, :].rearrange("p (k t) -> p k t", k=2))\
                        .then_inc(nat_hi, 1)

            def in_body(ph, i, first, evac_a, evac_b, nat, mid=None):
                for n_, (j, half, k0, n) in enumerate(units(8, 4)):
                    split(ph, i, j, half, n)
                    if n_ == 3:
                        if first and mid:
                            mid()
                        if not first and evac_b:
                            evac_b(i - 1)
                    if n_ == 11:
                        evac_a(i)
                        if nat and not first:
                            nat_evac_at(ph.nat0 + i - 1, i - 1)

            def out_phase(ph, kn, nat_last, gate=None, scale=1.0, mid=None):
                for b in range(4):
                    for n_, (j, half, k0, n) in enumerate(units(4, kn)):
                        split(ph, b, j, half, n)
                        if b == 0 and n_ == 3 and mid:
                            mid()
                        if b == 0 and n_ == 7:
                            nat_evac_at(nat_last, kn - 1)
                        if b == 1 and n_ == 3 and gate is not None:
                            for q in range(4):
                                act.wait_ge(gt_mm, 4 * gate + q + 1)
                                act.activation(gt_row[:, q * NC:(q + 1) * NC], (pr, pm)[q % 2][:, :],
                                               ACT.Copy, scale=scale).then_inc(gt_ok, 1)

            def turn_affine(kts, g0, scale, bias):
                for g in range(kts // 2):
                    act.wait_ge(xt_mm, g0 + g + 1)
                    if g0 + g >= 2:
                        act.wait_ge(xt_lo, g0 + g - 1)
                    if scale is None:
                        act.copy(buf_a[:, g % 2, :], px[:, g % 2, :]).then_inc(xt_f, 1)
                        continue
                    for k in (0, 1):
                        kt = 2 * g + k
                        ins = act.activation(buf_a[:, g % 2, k * T:(k + 1) * T], px[:, g % 2, k * T:(k + 1) * T],
                                             ACT.Identity, scale=scale(kt), bias=bias(kt))
                    ins.then_inc(xt_f, 1)

            def norm_stats(n, h_blocks):
                if n == 0:
                    act.wait_ge(x_in, 16)
                else:
                    act.wait_ge(h_ok, h_blocks)
                for tt in range(TT):
                    ins = act.activation(act_hi[:, 8 * tt:8 * tt + 8, :].rearrange("p k t -> p (k t)"), h[:, tt, :],
                                         ACT.Square, accum_out=st[:, 0, tt:tt + 1])
                ins.then_inc(ss_ok, 1)
                act.wait_ge(ss_ok, 2 * n + 2)
                act.activation(st[:, 2, :], st[:, 1, :], ACT.Sqrt).then_inc(rt_ok, 1)

            def norm(n, h_blocks, sh, g0):
                norm_stats(n, h_blocks)
                act.wait_ge(diag_ok, n + 1)
                turn_affine(KD, g0, lambda k: gain[:, k:k + 1], lambda k: mod[:, sh, k:k + 1])

            def silu(k):
                def run(i):
                    act.wait_ge(unit_used, 2 * (k.c0 + k.per * i) + 8)
                    if not (isinstance(i, int) and k.nat0 + i == 0):
                        act.wait_ge(nat_ok, k.nat0 + i)
                    act.activation(buf_a[:, :, :], pa[:, :, :], ACT.Silu).then_inc(pa_free, 1)
                return run

            def ffn(f, mid):
                for p, ng in enumerate(PARTS):
                    ph = plan[f"ffn{f}_in{p}"]
                    over(act, ng, lambda i, first: in_body(ph, i, first, silu(ph), None, True,
                                                           mid=mid if p == 0 else None))
                    name = f"ffn{f}_out{p}"
                    out_phase(plan[name], ng, ph.nat0 + ng - 1,
                              gate={"ffn1_out0": 0, "ffn2_out0": 2}.get(name), scale=0.5)

            act.wait_ge(par_ok, 1)
            act.activation(cond[:, :], par[:, PAR["c"]:PAR["c"] + KD], ACT.Silu).then_inc(cond_ok, 1)
            ffn(1, lambda: norm(0, 0, SH1, 0))

            def evac(ph, bank, free, after, dst, func, c0):
                def run(i):
                    act.wait_ge(consts, 2)
                    act.wait_ge(unit_used, 2 * (ph.c0 + ph.per * i) + after)
                    act.activation(dst[:, :, bass.ds(i * (2 * NC) + c0, NC)], bank[:, :, :], func)\
                        .then_inc(free, 1)
                return run
            ph = plan["proj"]
            pe_b = evac(ph, pb, pb_free, 16, proj, ACT.Copy, NC)
            over(act, 4, lambda i, first: in_body(ph, i, first, evac(ph, pa, pa_free, 8, proj, ACT.Copy, 0),
                                                  pe_b, False, mid=lambda: norm(1, 28 - 16, SH2, 8)))
            rp = plan["rest"]
            for n_, (j, half, k0, n) in enumerate(units(4, 4)):
                split(rp, 0, j, half, n, REST_W)
                if n_ == 3:
                    pe_b(3)
            gp = plan["gates"]

            def rest_evac():
                act.wait_ge(unit_used, 2 * rp.c0 + 8)
                act.copy(proj[:, :, 8 * NC:OG], pa[:, :, 0:REST_W]).then_inc(pa_free, 1)
            ge_b = evac(gp, pb, pb_free, 16, gates, ACT.Sigmoid, NC)
            over(act, 4, lambda i, first: in_body(gp, i, first, evac(gp, pa, pa_free, 8, gates, ACT.Sigmoid, 0),
                                                  ge_b, False, mid=rest_evac))
            ge_b(3)
            act.wait_ge(pa_free, gp.a0)
            act.activation(proj[:, :, OO:OG], proj[:, :, OO:OG], ACT.Sigmoid).then_inc(proj_ok, 1)

            act.wait_ge(rope_ang, 1)
            act.activation(ang[:, 6:8, :, :], ang[:, 4:6, :, :], ACT.Sin).then_inc(trig_ok, 1)
            act.wait_ge(kt_mm, 1)
            act.copy(k_t[:, :, :], px[0:HD, 0, :].rearrange("p (g t) -> p g t", g=KV)).then_inc(kt_ok, 1)

            NPAIR = HQ // KV // 2

            def pair(n):
                act.wait_ge(rope_ok, 1)
                act.copy(q_st[:, :, :], proj[:, :, bass.ds(n * (2 * HD), 2 * HD)]).then_inc(q_in, 1)
                act.wait_ge(q_mm, n + 1)
                act.copy(q_t[:, 0, :], px[0:HD, 0, 0:T])
                act.copy(q_t[:, 1, :], px[HD:2 * HD, 0, 0:T]).then_inc(q_ok, 1)
                act.wait_ge(mx_ok, n + 1)
                act.activation(m_st[:, 6, :], m_st[:, 5, :], ACT.Exp)
                for hh in (0, 1):
                    for b, cols in ((0, slice(0, P)), (1, slice(P, 3 * P))):
                        o = 2 * b + hh
                        ins = act.activation(s_sb[:, hh, cols], s_sb[:, hh, cols], ACT.Exp,
                                             bias=m_st[:, 4, o:o + 1], accum_out=m_st[:, 7, o:o + 1])
                ins.then_inc(p_ok, 1)
                act.wait_ge(pt_mm, n + 1)
                act.copy(p_t[:, :, :, :], pb[:, :, 0:3 * P].rearrange("p a (b t) -> p a b t", b=3))\
                    .then_inc(pt_ok, 1)
            for g in range(KV):
                with act.Fori(0, NPAIR) as i:
                    pair(i + g * NPAIR)

            act.wait_ge(g_abs, 1)
            link(act.activation(m_st[:, 10:12, :], m_st[:, 8:10, :], ACT.Exp, scale=-1.0))
            act.activation(m_st[:, 8:10, :], m_st[:, 10:12, :], ACT.Ln, bias=1.0).then_inc(g_ln, 1)
            for tt in range(TT):
                act.wait_ge(g_row, tt + 1)
                act.copy(r_row[:, :, tt * P:(tt + 1) * P],
                         (pr if tt == 0 else pm)[:, :].rearrange("p (a t) -> p a t", a=MH)).then_inc(g_rowok, 1)
            for hd in range(MH):
                act.wait_ge(m_tr, hd + 1)
                act.copy(xpad[:, :, CONV - 1:], px[:, 0, :].rearrange("p (a t) -> p a t", a=2)).then_inc(m_pad, 1)
                act.wait_ge(m_conv, hd + 1)
                for qk in (0, 1):
                    cb = PAR["conv_b"] + qk * MH + hd
                    ins = act.activation(mq_t[:, qk, :], mq_t[:, qk, :], ACT.Silu, bias=par[:, cb:cb + 1])
                ins.then_inc(m_qk, 1)
                act.wait_ge(m_max, hd + 1)
                act.activation(w_sb[:, 0:P], w_sb[:, 0:P], ACT.Exp, bias=m_st[:, 12, 0:1])
                act.activation(w_sb[:, P:3 * P], w_sb[:, P:3 * P], ACT.Exp, bias=m_st[:, 12, 1:2])
                act.activation(m_st[:, 13, 0:2], m_st[:, 13, 2:4], ACT.Exp).then_inc(m_w, 1)
                act.wait_ge(m_at, hd + 1)
                act.copy(a_t[:, :, :], pb[:, 0, 0:3 * P].rearrange("p (b t) -> p b t", b=3)).then_inc(m_atok, 1)
                act.wait_ge(m_h, hd + 1)
                for tt in range(TT):
                    ins = act.activation((w_sb, a_sb)[tt][:, 0:MV], hm[:, tt, :], ACT.Square, accum_out=m_st[:, 14, tt:tt + 1])
                ins.then_inc(m_ss, 1)
                act.wait_ge(m_var, hd + 1)
                act.activation(m_st[:, 15, 0:2], m_st[:, 14, 2:4], ACT.Sqrt).then_inc(m_rt, 1)
            turn_affine(ATT // P, 16, None, None)
            turn_affine(MW // P, 20, lambda k: par[:, PAR["mg"] + k:PAR["mg"] + k + 1], lambda k: 0.0)

            ph = plan["up"]

            def up(i, first):
                for n_, (j, half, k0, n) in enumerate(units(4, 4)):
                    split(ph, i, j, half, n)
                if not first:
                    nat_evac_at(ph.nat0 + i - 1, i - 1)
            over(act, 4, up)
            out_phase(plan["wout"], 4, ph.nat0 + 3, gate=1)
            ffn(2, lambda: norm(2, 28 - 12, SH3, 24))
            norm_stats(3, 28)

        @block.vector
        def _(dve):
            steps = [0]

            def link(ins):
                steps[0] += 1
                ins.then_inc(dve_step, 1)
                dve.wait_ge(dve_step, steps[0])

            def split(ph, i, j, half, n, w=NC):
                u = 2 * (ph.c0 + ph.per * i + j) + half
                dve.wait_ge(hi_done, u + 1)
                s = slice(2 * half, 2 * half + n)
                dve.tensor_tensor(lo[:, j % RING, s, 0:w], raw[:, j % RING, s, 0:w],
                                  hi[:, (2 * j + half) % 4, 0:n, 0:w].bitcast(F32), ALU.subtract)\
                    .then_inc(lo_done, 1)

            def ada(name, i, j):
                m, k0, n = ada_plan[name]
                per = plan[name].per if name in plan else 8
                tile = ada_first[name] + per * i + j
                kt = k0 + (per // 2) * i + j // 2
                half = j % 2
                dve.wait_ge(ada_in[j % ADA_RING], 16 * (ada_first[name] // ADA_RING + (per // ADA_RING) * i
                                                        + j // ADA_RING + 1))
                wt = ada_w[:, j % ADA_RING, :]
                acc = ada_acc[:, half, :]
                if isinstance(kt, int) and kt == 0:
                    if m > 0:
                        dve.wait_ge(flushed, m)
                    dve.tensor_scalar(acc, wt, cond[:, 0:1], None, ALU.mult).then_inc(ada_done, 1)
                    return
                dve.wait_ge(ada_done, tile - 1)
                dve.scalar_tensor_tensor(out=acc, in0=wt, scalar=cond[:, bass.ds(kt, 1)], in1=acc,
                                         op0=ALU.mult, op1=ALU.add).then_inc(ada_done, 1)

            def mod_row(m):
                dve.wait_ge(flushed, m + 1)
                dve.tensor_tensor(mod[:, m, :], pm[:, 0:KD], bada[:, m * KD:(m + 1) * KD], ALU.add)\
                    .then_inc(mod_ok, 1)

            def nat_evac(nb, slot):
                for b in (0, 1):
                    dve.wait_ge(nat_hi, 2 * nb + b + 1)
                    k = 4 * slot + 2 * b
                    dve.tensor_tensor(hid_lo[:, bass.ds(k, 2), :], px[:, b, :].rearrange("p (k t) -> p k t", k=2),
                                      hid_hi[:, bass.ds(k, 2), :].bitcast(F32), ALU.subtract).then_inc(nat_lo, 1)

            def hidden(ph, i):
                dve.wait_ge(unit_used, 2 * (ph.c0 + ph.per * (i + 1)))
                dve.wait_ge(pa_free, ph.a0 + i + 1)
                dve.tensor_tensor(buf_b[:, :, :], buf_a[:, :, :], pb[:, :, :], ALU.mult)\
                    .then_inc(nat_ok, 1)

            def ffn_in(name, ng, mid, pb_inc):
                ph = plan[name]

                def body(i, first):
                    for n_, (j, half, k0, n) in enumerate(units(8, 4)):
                        split(ph, i, j, half, n)
                        if n_ == 3:
                            if first and mid:
                                mid()
                            if not first:
                                hidden(ph, i - 1)
                        if n_ == 11 and not first:
                            nat_evac(ph.nat0 + i - 1, i - 1)
                        if half == 1 and name in ada_plan:
                            ada(name, i, j)
                over(dve, ng, body)

            def add_out(ph, b, out_i, gate):
                bank, free = (pa, pa_free) if b % 2 == 0 else (pb, pb_free)
                dve.wait_ge(unit_used, 2 * (ph.c0 + ph.per * (b + 1)))
                if b == 0:
                    dve.wait_ge(gt_ok, 4 * gate + 4)
                row = gt_row[:, b * NC:(b + 1) * NC].unsqueeze(1).broadcast_to([P, TT, NC])
                dve.tensor_tensor(buf_a[:, :, :], bank[:, :, :], row, ALU.mult).then_inc(free, 1)
                use = (ph.a0 if b % 2 == 0 else ph.b0) + b // 2 + 1
                dve.wait_ge(free, use)
                hs = h[:, :, b * NC:(b + 1) * NC]
                dve.tensor_tensor(hs, hs, buf_a[:, :, :], ALU.add).then_inc(h_ok, 1)

            def out_phase(name, kn, nat_last, hid_tail, out_i, gate, flush_m=None, diag_m=None):
                ph = plan[name]
                for b in range(4):
                    for n_, (j, half, k0, n) in enumerate(units(4, kn)):
                        split(ph, b, j, half, n)
                        if n_ == 3:
                            if b == 0:
                                hid_tail()
                            else:
                                add_out(ph, b - 1, out_i, gate)
                        if n_ == 7 and b == 0:
                            nat_evac(nat_last, kn - 1)
                            if flush_m is not None:
                                mod_row(flush_m)
                            if diag_m is not None:
                                dve.wait_ge(mod_ok, diag_m + 1)
                                col = mod[:, diag_m, :].unsqueeze(2).broadcast_to([P, KD, P])
                                idb = ident[:, :].unsqueeze(1).broadcast_to([P, KD, P])
                                dve.tensor_tensor(gt_row[:, :].rearrange("p (k q) -> p k q", k=KD), idb, col,
                                                  ALU.mult).then_inc(gt_diag, 1)
                        if half == 1 and name in ada_plan:
                            ada(name, b, j)
                return lambda: add_out(ph, 3, out_i, gate)

            def rstd(n):
                dve.wait_ge(ss_ok, 2 * n + 1)
                dve.tensor_scalar(st[:, 1, :], st[:, 0, :], 1.0 / D, EPS, ALU.mult, ALU.add).then_inc(ss_ok, 1)
                dve.wait_ge(rt_ok, n + 1)
                link(dve.reciprocal(st[:, 3, :], st[:, 2, :]))
                newton(st[:, 3, :], st[:, 1, :], st[:, 4, :], st[:, 5, :], st[:, 6, :])

            def newton(r, v, t0, t1, res):
                link(dve.tensor_tensor(t0, r, r, ALU.mult))
                link(dve.tensor_tensor(t1, t0, v, ALU.mult))
                link(dve.tensor_scalar(t1, t1, -0.5, 1.5, ALU.mult, ALU.add))
                link(dve.tensor_tensor(res, r, t1, ALU.mult))

            def turn_split(kts, g0, kdst):
                for g in range(kts // 2):
                    dve.wait_ge(xt_f, g0 + g + 1)
                    src = buf_a[:, g % 2, :].rearrange("p (k t) -> p k t", k=2)
                    ks = slice(kdst + 2 * g, kdst + 2 * g + 2)
                    dve.tensor_copy(act_hi[:, ks, :], src).then_inc(xt_hi, 1)
                    dve.wait_ge(xt_hi, g0 + g + 1)
                    dve.tensor_tensor(act_lo[:, ks, :], src, act_hi[:, ks, :].bitcast(F32), ALU.subtract)\
                        .then_inc(xt_lo, 1)

            def norm(n, sc, g, g0):
                rstd(n)
                for tt in range(TT):
                    dve.tensor_scalar(dg[:, tt, :], ident[:, :], st[:, 6, tt:tt + 1], None, ALU.mult)
                dve.wait_ge(mod_ok, sc + 1)
                dve.scalar_tensor_tensor(out=gain[:, :], in0=mod[:, sc, :], scalar=1.0,
                                         in1=par[:, PAR[g]:PAR[g] + KD], op0=ALU.add, op1=ALU.mult)\
                    .then_inc(diag_ok, 1)
                turn_split(KD, g0, 0)

            def ffn(f, mid, out0):
                for p, ng in enumerate(PARTS):
                    name = f"ffn{f}_in{p}"
                    ph = plan[name]
                    ffn_in(name, ng, mid, True)
                    oname = f"ffn{f}_out{p}"
                    mid = out_phase(oname, ng, ph.nat0 + ng - 1, lambda: hidden_last(ph, ng - 1),
                                    out0 + p, 0 if f == 1 else 2,
                                    flush_m={"ffn1_out0": GT1, "ffn1_out1": SH2, "ffn2_out0": GT3}.get(oname),
                                    diag_m={"ffn1_out0": GT1, "ffn2_out0": GT3}.get(oname))
                return mid

            def hidden_last(ph, i):
                hidden(ph, i)

            for i in range(HALF):
                dve.memset(inv_f[:, i:i + 1], float(np.float32(ROPE_THETA ** (-i * 2.0 / ROT))))
            dve.wait_ge(par_tr, 1)
            dve.tensor_copy(par[:, 0:NPAR], px[:, 0, 0:NPAR]).then_inc(par_ok, 1)
            dve.tensor_copy(bada[:, :], px[:, 0, P:P + NB]).then_inc(par_ok, 1)
            dve.wait_ge(par_ok, 2)
            dve.wait_ge(cond_ok, 1)
            for m, name in ((SH1, "start0"), (SC1, "start1")):
                over(dve, 4, lambda i, first: [ada(name, i, j) for j in range(8)])
                mod_row(m)
            tail = ffn(1, lambda: norm(0, SC1, "g1", 0), 0)

            def mid2():
                tail()
                mod_row(SC2)
                norm(1, SC2, "g2", 8)
            for name in ("proj", "rest", "gates"):
                ph = plan[name]

                def body(i, first):
                    for n_, (j, half, k0, n) in enumerate(units(ph.per, 4)):
                        split(ph, i, j, half, n, REST_W if name == "rest" else NC)
                        if first and n_ == 3 and name == "proj":
                            mid2()
                        if half == 1 and name in ada_plan:
                            ada(name, i, j)
                over(dve, ph.n, body)
                if name == "rest":
                    mod_row(GT2)
            mod_row(SH3)

            dve.wait_ge(rows_in, 64)
            link(dve.tensor_copy(st[:, 7, :], pos_i[:, :]))
            base = ang[:, 0, :, :]
            link(dve.tensor_tensor(base, st[:, 7, :].unsqueeze(2).broadcast_to([P, TT, HALF]),
                                   inv_f[:, :].unsqueeze(1).broadcast_to([P, TT, HALF]), ALU.mult))
            dve.tensor_scalar(ang[:, 2, :, :], base, 1.0 / (2 * np.pi), None, ALU.mult)
            link(dve.tensor_scalar(ang[:, 3, :, :], base, 1.0 / (2 * np.pi), 0.25, ALU.mult, ALU.add))
            link(dve.tensor_scalar(ang[:, 2:4, :, :], ang[:, 2:4, :, :], ROUND_MAGIC, None, ALU.add))
            link(dve.tensor_scalar(ang[:, 2:4, :, :], ang[:, 2:4, :, :], ROUND_MAGIC, None, ALU.subtract))
            for part in (TWO_PI_A, TWO_PI_B, TWO_PI_C):
                src = (base, base) if part == TWO_PI_A else (ang[:, 4, :, :], ang[:, 5, :, :])
                dve.scalar_tensor_tensor(out=ang[:, 4, :, :], in0=ang[:, 2, :, :], scalar=-part, in1=src[0],
                                         op0=ALU.mult, op1=ALU.add)
                link(dve.scalar_tensor_tensor(out=ang[:, 5, :, :], in0=ang[:, 3, :, :], scalar=-part, in1=src[1],
                                              op0=ALU.mult, op1=ALU.add))
            link(dve.tensor_scalar(ang[:, 5, :, :], ang[:, 5, :, :], float(np.pi / 2), None, ALU.add))
            dve.tensor_scalar(ang[:, 4:6, :, :], ang[:, 4:6, :, :], 3.1415925, -3.1415925, ALU.min, ALU.max)\
                .then_inc(rope_ang, 1)
            dve.wait_ge(trig_ok, 1)
            dve.wait_ge(proj_ok, 1)
            HR = HQ + KV
            for tt in range(TT):
                qk = proj[:, tt, 0:OV].rearrange("p (h d) -> p h d", d=HD)
                x1, x2 = qk[:, :, 0:HALF], qk[:, :, HALF:ROT]
                sin = ang[:, 6, tt, :].unsqueeze(1).broadcast_to([P, HR, HALF])
                cos = ang[:, 7, tt, :].unsqueeze(1).broadcast_to([P, HR, HALF])
                r = [rope_t[:, k, :].rearrange("p (h d) -> p h d", d=HALF) for k in range(4)]
                dve.tensor_tensor(r[0], x1, cos, ALU.mult)
                dve.tensor_tensor(r[1], x2, sin, ALU.mult)
                dve.tensor_tensor(r[2], x2, cos, ALU.mult)
                link(dve.tensor_tensor(r[3], x1, sin, ALU.mult))
                dve.tensor_tensor(x1, r[0], r[1], ALU.subtract)
                link(dve.tensor_tensor(x2, r[2], r[3], ALU.add))
            dve.memset(xpad[:, :, 0:CONV - 1], 0.0).then_inc(rope_ok, 1)

            NPAIR = HQ // KV // 2
            LINKS = 5
            base_step = steps[0]

            def pair(n):
                k = [0]

                def chain(ins):
                    k[0] += 1
                    ins.then_inc(dve_step, 1)
                    dve.wait_ge(dve_step, base_step + n * LINKS + k[0])

                dve.wait_ge(sc_mm, n + 1)
                own = mask[:, P:2 * P].unsqueeze(1).broadcast_to([P, 2, P])
                both = mask[:, :].unsqueeze(1).broadcast_to([P, 2, 2 * P])
                dve.scalar_tensor_tensor(out=s_sb[:, :, 0:P], in0=pa[:, 0, 0:2 * P].rearrange("p (a t) -> p a t", a=2),
                                         scalar=HD ** -0.5, in1=own, op0=ALU.mult, op1=ALU.add)
                chain(dve.scalar_tensor_tensor(out=s_sb[:, :, P:3 * P],
                                               in0=pa[:, 1, :].rearrange("p (a t) -> p a t", a=2),
                                               scalar=HD ** -0.5, in1=both, op0=ALU.mult, op1=ALU.add))
                dve.tensor_reduce(m_st[:, 2, 0:2], s_sb[:, :, 0:P], AX.X, ALU.max)
                chain(dve.tensor_reduce(m_st[:, 2, 2:4], s_sb[:, :, P:3 * P], AX.X, ALU.max))
                sink = sink_row[:, bass.ds(n * 2, 2)].unsqueeze(1).broadcast_to([P, 2, 2])
                mx = m_st[:, 3, :].rearrange("p (b a) -> p b a", b=2)
                chain(dve.tensor_tensor(mx, m_st[:, 2, :].rearrange("p (b a) -> p b a", b=2), sink, ALU.max))
                dve.tensor_tensor(m_st[:, 5, :].rearrange("p (b a) -> p b a", b=2), sink, mx, ALU.subtract)
                dve.tensor_scalar(m_st[:, 4, :], m_st[:, 3, :], -1.0, None, ALU.mult).then_inc(mx_ok, 1)
                dve.wait_ge(p_ok, n + 1)
                chain(dve.tensor_tensor(m_st[:, 7, :], m_st[:, 7, :], m_st[:, 6, :], ALU.add))
                chain(dve.reciprocal(m_st[:, 7, :], m_st[:, 7, :]))
                dve.wait_ge(o_mm, n + 1)
                for b in range(TT):
                    dst = proj[:, b, bass.ds(n * (2 * HD), 2 * HD)].rearrange("p (a d) -> p a d", a=2)
                    src = px[:, 1, 2 * b * HD:2 * (b + 1) * HD].rearrange("p (a d) -> p a d", a=2)
                    ins = dve.tensor_tensor(dst, src, m_st[:, 7, 2 * b:2 * b + 2].unsqueeze(2).broadcast_to([P, 2, HD]),
                                            ALU.mult)
                ins.then_inc(o_ok, 1)
            for g in range(KV):
                with dve.Fori(0, NPAIR) as i:
                    pair(i + g * NPAIR)
            steps[0] = base_step + KV * NPAIR * LINKS

            f_raw = proj[:, :, OF:OF + MH]
            link(dve.tensor_tensor(m_st[:, 4:6, :], f_raw, gb_row[:, 1, :].unsqueeze(1).broadcast_to([P, TT, MH]),
                                   ALU.add))
            dve.tensor_scalar(m_st[:, 0:2, :], m_st[:, 4:6, :], 0.0, None, ALU.min)
            link(dve.tensor_scalar(m_st[:, 6:8, :], m_st[:, 4:6, :], -1.0, None, ALU.mult))
            dve.tensor_tensor(m_st[:, 8:10, :], m_st[:, 4:6, :], m_st[:, 6:8, :], ALU.max).then_inc(g_abs, 1)
            dve.wait_ge(g_ln, 1)
            dve.tensor_tensor(m_st[:, 0:2, :], m_st[:, 0:2, :], m_st[:, 8:10, :], ALU.subtract).then_inc(g_logf, 1)
            dve.wait_ge(g_cum, 1)
            dve.tensor_copy(m_st[:, 2:4, :], pm[:, 0:2 * MH].rearrange("p (t a) -> p t a", t=TT))
            link(dve.tensor_tensor(m_st[:, 6:8, :], proj[:, :, OI:OI + MH],
                                   gb_row[:, 0, :].unsqueeze(1).broadcast_to([P, TT, MH]), ALU.add))
            link(dve.tensor_tensor(m_st[:, 4:6, :], m_st[:, 6:8, :], m_st[:, 2:4, :], ALU.subtract))
            for tt in range(TT):
                if tt == 1:
                    dve.wait_ge(g_row, 1)
                dve.tensor_tensor(dg[:, :, :], ident[:, :].unsqueeze(1).broadcast_to([P, MH, P]),
                                  m_st[:, 4 + tt, :].unsqueeze(2).broadcast_to([P, MH, P]), ALU.mult)\
                    .then_inc(g_diag, 1)
            dve.wait_ge(g_rowok, 2)
            for hd in range(MH):
                if hd > 0:
                    dve.wait_ge(m_rt, hd)
                dve.tensor_tensor(w_sb[:, 0:P], r_row[:, hd, 0:P], mask[:, P:2 * P], ALU.add)
                dve.tensor_copy(w_sb[:, P:2 * P], r_row[:, hd, 0:P])
                link(dve.tensor_tensor(w_sb[:, 2 * P:3 * P], r_row[:, hd, P:T], mask[:, P:2 * P], ALU.add))
                dve.tensor_reduce(m_st[:, 12, 2:3], w_sb[:, 0:P], AX.X, ALU.max)
                link(dve.tensor_reduce(m_st[:, 12, 3:4], w_sb[:, P:3 * P], AX.X, ALU.max))
                link(dve.tensor_scalar(m_st[:, 12, 0:2], m_st[:, 12, 2:4], -1.0, None, ALU.mult))
                dve.tensor_tensor(m_st[:, 13, 2:4], m_st[:, 12, 0:2],
                                  m_st[:, 2:4, hd], ALU.subtract).then_inc(m_max, 1)
                dve.wait_ge(m_pad, hd + 1)
                for s in range(CONV):
                    for qk in (0, 1):
                        cw = PAR["conv_w"] + s * (MQK2 // P) + qk * MH + hd
                        src = xpad[:, qk, s:s + T]
                        if s == 0:
                            ins = dve.tensor_scalar(mq_t[:, qk, :], src, par[:, cw:cw + 1], None, ALU.mult)
                        else:
                            ins = dve.scalar_tensor_tensor(out=mq_t[:, qk, :], in0=src, scalar=par[:, cw:cw + 1],
                                                           in1=mq_t[:, qk, :], op0=ALU.mult, op1=ALU.add)
                    if s < CONV - 1:
                        link(ins)
                ins.then_inc(m_conv, 1)
                dve.wait_ge(m_sc, hd + 1)
                dve.wait_ge(m_w, hd + 1)
                dve.scalar_tensor_tensor(out=a_sb[:, 0:P], in0=pa[:, 0, 0:P], scalar=DK ** -0.5, in1=w_sb[:, 0:P],
                                         op0=ALU.mult, op1=ALU.mult, accum_out=m_st[:, 10, 0:1])
                ins = dve.scalar_tensor_tensor(out=a_sb[:, P:3 * P], in0=pa[:, 0, P:3 * P], scalar=DK ** -0.5,
                                               in1=w_sb[:, P:3 * P], op0=ALU.mult, op1=ALU.mult,
                                               accum_out=m_st[:, 10, 1:2])
                ins.then_inc(m_a, 1)
                dve.wait_ge(m_a, hd + 1)
                link(dve.tensor_scalar(m_st[:, 11, 0:2], m_st[:, 10, 0:2], -1.0, None, ALU.mult))
                link(dve.tensor_tensor(m_st[:, 11, 0:2], m_st[:, 10, 0:2], m_st[:, 11, 0:2], ALU.max))
                link(dve.tensor_tensor(m_st[:, 11, 0:2], m_st[:, 11, 0:2], m_st[:, 13, 0:2], ALU.max))
                link(dve.reciprocal(m_st[:, 11, 0:2], m_st[:, 11, 0:2]))
                dve.wait_ge(m_num, hd + 1)
                for tt in range(TT):
                    ins = dve.tensor_scalar(hm[:, tt, :], px[:, 1, tt * MV:(tt + 1) * MV],
                                            m_st[:, 11, tt:tt + 1], None, ALU.mult)
                ins.then_inc(m_h, 1)
                dve.wait_ge(m_ss, hd + 1)
                dve.tensor_scalar(m_st[:, 14, 2:4], m_st[:, 14, 0:2], 1.0 / MV, EPS, ALU.mult, ALU.add)\
                    .then_inc(m_var, 1)
                dve.wait_ge(m_rt, hd + 1)
                dve.wait_ge(m_var, hd + 1)
                link(dve.reciprocal(m_st[:, 15, 2:4], m_st[:, 15, 0:2]))
                newton(m_st[:, 15, 2:4], m_st[:, 14, 2:4], m_st[:, 10, 0:2], m_st[:, 10, 2:4], m_st[:, 11, 0:2])
                for tt in range(TT):
                    vs = slice(OMV + hd * MV, OMV + (hd + 1) * MV)
                    os = slice(OO + hd * MV, OO + (hd + 1) * MV)
                    ins = dve.scalar_tensor_tensor(out=proj[:, tt, vs], in0=hm[:, tt, :],
                                                   scalar=m_st[:, 11, tt:tt + 1], in1=proj[:, tt, os],
                                                   op0=ALU.mult, op1=ALU.mult)
                ins.then_inc(m_out, 1)
            turn_split(ATT // P, 16, 0)
            turn_split(MW // P, 20, 8)

            ph = plan["up"]

            def mix_a(i):
                dve.wait_ge(unit_used, 2 * (ph.c0 + ph.per * i) + 4)
                dve.tensor_tensor(buf_a[:, :, :], pa[:, :, :], gates[:, :, bass.ds(i * NC, NC)], ALU.mult)\
                    .then_inc(pa_free, 1)

            def mix_b(i):
                dve.wait_ge(unit_used, 2 * (ph.c0 + ph.per * i) + 8)
                dve.tensor_tensor(buf_b[:, :, :], pb[:, :, :], gates[:, :, bass.ds(i * NC + D, NC)], ALU.mult)\
                    .then_inc(pb_free, 1)
                dve.wait_ge(pb_free, ph.b0 + i + 1)
                dve.wait_ge(pa_free, ph.a0 + i + 1)
                dve.tensor_tensor(buf_b[:, :, :], buf_b[:, :, :], buf_a[:, :, :], ALU.add).then_inc(nat_ok, 1)

            def up(i, first):
                for n_, (j, half, k0, n) in enumerate(units(4, 4)):
                    split(ph, i, j, half, n)
                    if n_ == 3 and not first:
                        mix_b(i - 1)
                    if half == 1:
                        ada("up", i, j)
                mix_a(i)
                if not first:
                    nat_evac(ph.nat0 + i - 1, i - 1)
            over(dve, 4, up)
            tail2 = out_phase("wout", 4, ph.nat0 + 3, lambda: mix_b(3), 3, 1, diag_m=GT2)

            def mid3():
                tail2()
                mod_row(SC3)
                norm(2, SC3, "g3", 24)
            ffn(2, mid3, 4)()
            rstd(3)
            dve.wait_ge(fin_in, 16)
            for tt in range(TT):
                dve.scalar_tensor_tensor(out=h[:, tt, :], in0=h[:, tt, :], scalar=st[:, 6, tt:tt + 1],
                                         in1=fin_row[:, :], op0=ALU.mult, op1=ALU.mult).then_inc(fin_ok, 1)


_INS = ['x', 'c', 'positions', 'w_ada', 'b_ada', 'norm1_g', 'ffn1_w_in', 'ffn1_w_out', 'norm2_g', 'w_in',
        'conv_w', 'conv_b', 'b_igate', 'b_fgate', 'sinks', 'mlstm_norm_g', 'w_att_up', 'w_mlstm_up',
        'w_out', 'norm3_g', 'ffn2_w_in', 'ffn2_w_out', 'final_g']


def kernel(**inputs):
    import numpy as _np
    import concourse.bacc as _bacc
    from concourse import mybir as _mybir
    from concourse.bass_utils import run_bass_kernel_spmd as _run

    nc = _bacc.Bacc("TRN2", target_bir_lowering=False, num_devices=1)
    arrays, args = {}, []
    for name in _INS:
        a = _np.ascontiguousarray(inputs[name])
        arrays[f"in_{name}_dram"] = a
        args.append(nc.dram_tensor(f"in_{name}_dram", a.shape, _mybir.dt.from_np(a.dtype), kind="ExternalInput").ap())
    shape = inputs["x"].shape
    args.append(nc.dram_tensor("out_0_dram", shape, _mybir.dt.float32, kind="ExternalOutput").ap())
    build(nc, *args)
    r = _run(nc, [arrays], core_ids=[0])
    return r.results[0]["out_0_dram"]
```

```python
from contextlib import ExitStack

import numpy as np
import concourse.bass as bass
from concourse import mybir

F32 = mybir.dt.float32
F32R = mybir.dt.float32r
I32 = mybir.dt.int32
ALU = mybir.AluOpType
ACT = mybir.ActivationFunctionType
AX = mybir.AxisListType

P = 128
NC = 512
RING = 4
ADA_RING = 4
ADA_W = 1024
EPS = 1e-6
NEG = -1e30
ROPE_THETA = 500000.0
WINDOW = 128
TWO_PI_A = 6.28125
TWO_PI_B = float(np.float32(np.floor((2 * np.pi - 6.28125) * 2 ** 20) / 2 ** 20))
TWO_PI_C = float(2 * np.pi - 6.28125 - TWO_PI_B)
ROUND_MAGIC = 12582912.0


class Phase:

    def __init__(self, n, per, c0, a0, b0, nat0):
        self.n, self.per, self.c0, self.a0, self.b0, self.nat0 = n, per, c0, a0, b0, nat0


def build(nc, x, c, positions, w_ada, b_ada, norm1_g, ffn1_w_in, ffn1_w_out, norm2_g, w_in,
          conv_w, conv_b, b_igate, b_fgate, sinks, mlstm_norm_g, w_att_up, w_mlstm_up, w_out,
          norm3_g, ffn2_w_in, ffn2_w_out, final_g, out):
    T, D = x.shape[1], x.shape[2]
    TT = T // P
    KD = D // P
    FF = ffn1_w_out.shape[1]
    HQ = sinks.shape[1]
    ATT = w_att_up.shape[1]
    HD = ATT // HQ
    MH = b_igate.shape[1]
    MW = w_mlstm_up.shape[1]
    MV = MW // MH
    MQK2 = conv_w.shape[2]
    DK = MQK2 // (2 * MH)
    CONV = conv_w.shape[1]
    KVW = (w_in.shape[2] - ATT - MQK2 - 2 * MW - 2 * MH - 2 * D) // 2
    KV = KVW // HD
    OK = ATT
    OV = OK + KVW
    OM = OV + KVW
    OMV = OM + MQK2
    OI = OMV + MW
    OF = OI + MH
    OO = OF + MH
    OG = OO + MW
    ROT = HD // 4
    HALF = ROT // 2
    assert TT == 2 and KD == 16 and DK == P and WINDOW == P and MV == 2 * P and KV == 2

    PARTS = (4, 4, 3)
    assert sum(PARTS) * NC == FF
    plan = {}
    total = [0, 0, 0, 0]

    def plan_phase(name, iters, chunks, a, b, nat=0):
        plan[name] = Phase(iters, chunks, *total)
        for k, more in enumerate((iters * chunks, a, b, nat)):
            total[k] += more

    def plan_ffn(f):
        for p, g in enumerate(PARTS):
            plan_phase(f"ffn{f}_in{p}", g, 8, g, 0, g)
            plan_phase(f"ffn{f}_out{p}", 4, 4, 2, 2)

    plan_ffn(1)
    plan_phase("proj", 4, 8, 4, 4)
    plan_phase("rest", 1, 4, 1, 0)
    plan_phase("gates", 4, 8, 4, 4)
    plan_phase("up", 4, 4, 4, 4, 4)
    plan_phase("wout", 4, 4, 2, 2)
    plan_ffn(2)
    REST_W = OG - 8 * NC
    ADA = {"start0": ("pair", 0), "start1": ("pair", 2), "ffn1_in0": ("pair", 4), "ffn1_out0": ("one", 6),
           "ffn1_in1": ("pair", 7), "ffn1_out1": ("one", 9), "ffn1_in2": ("late", 10), "ffn1_out2": ("one", 11),
           "proj": ("pair", 12), "up": ("one", 14), "wout": ("one", 15), "ffn2_in0": ("pair", 16)}
    ada_first = {}
    flush_at = []
    tiles_of = []
    t = 0
    for name, (kind, first) in ADA.items():
        ada_first[name] = t
        halves = 2 if kind == "pair" else 1
        t += halves * KD
        flush_at.append((first, halves))
        tiles_of.append(t)

    def flush_no(half_row):
        return next(k for k, (first, n) in enumerate(flush_at) if first <= half_row < first + n)

    def ada_tile(name, i, j):
        kind, first = ADA[name]
        if kind == "pair":
            return ada_first[name] + 8 * i + j, first + j % 2, 4 * i + j // 2
        if kind == "one":
            return ada_first[name] + 4 * i + j, first, 4 * i + j
        if isinstance(i, int) and i == 0:
            return None
        return ada_first[name] + 8 * (i - 1) + j, first, 8 * (i - 1) + j
    GROUPS_AT = {3: (0, 1, 2), 4: (3,), 5: (4,), 6: (5,), 7: (6, 7)}
    FIRST_AT = {0: (0, 1), 1: (2,), 2: (3,), 8: (4, 5), 9: (6,), 10: (7,)}
    FIRST_TILES = {5: range(4), 6: (4, 5), 7: (6, 7)}
    START1_TILES = {0: range(2), 1: range(2, 5), 2: range(5, 8), 3: range(8, 10), 4: range(10, 13),
                    5: range(13, 16), 6: range(16, 19), 7: range(19, 32)}
    OUT_AT = {1: (0, 1), 3: (2,), 4: (3,), 5: (4,), 6: (5,), 7: (6, 7)}
    FIRST_CHUNKS = (0, 1, 4, 5, 2, 3, 6, 7)
    ROW = (0, 2, 1, 3, *range(4, 18))
    SH1, SC1, GT1, SH2, SC2, GT2, SH3, SC3, GT3 = range(9)

    with ExitStack() as ctx:
        def sb(name, shape, dt=F32):
            return ctx.enter_context(nc.sbuf_tensor(name, shape, dt))

        def psum(name, shape):
            return ctx.enter_context(nc.psum_tensor(name, shape, F32))

        def sem(name):
            return ctx.enter_context(nc.semaphore(name))

        h = sb("h", [P, TT, D])
        with nc.sbuf_tensor("raw", [P, RING, 4, NC], F32) as raw:
            pass
        lo = sb("lo", [P, RING, 4, NC], F32R)
        hi = sb("hi", [P, RING, 2, NC], F32R)
        act_hi = sb("act_hi", [P, KD, T], F32R)
        act_lo = sb("act_lo", [P, KD, T], F32R)

        def shared(*groups):
            out = []
            for g in groups:
                with ExitStack() as inner:
                    out.append([inner.enter_context(nc.sbuf_tensor(*t)) for t in g])
            size = max(sum(int(np.prod(t[1][1:])) for t in g) for g in groups)
            sb("at_" + groups[0][0][0], [P, size])
            return out

        (ada_w,), (s_sb, p_t, q_st, q_t, k_g, mq_t, w_sb, a_t) = shared(
            [("ada_w", [P, ADA_RING, ADA_W], F32)],
            [("s_sb", [P, 2, 3 * P], F32), ("p_t", [P, 2, 3, P], F32), ("q_st", [P, TT, 2 * HD], F32),
             ("q_t", [HD, 2, T], F32), ("k_g", [HD, T], F32), ("mq_t", [P, 2, T], F32), ("w_sb", [P, 3 * P], F32),
             ("a_t", [P, 3, P], F32)])
        (ada_acc,), (r_row, dgm) = shared(
            [("ada_acc", [P, 2, ADA_W], F32)],
            [("r_row", [P, MH, T], F32), ("dgm", [P, TT, MH, P], F32)])
        (buf_a, buf_b), (k_t, xpad, rope_t), (par_in, bada_in) = shared(
            [("buf_a", [P, TT, NC], F32), ("buf_b", [P, TT, NC], F32)],
            [("k_t", [HD, KV, T], F32), ("xpad", [P, 2, CONV - 1 + T], F32),
             ("rope_t", [P, 4, (HQ + KV) * HALF], F32)],
            [("par_in", [P, P], F32), ("bada_in", [P, 2, P], F32)])
        ident = sb("ident", [P, P])
        ones = sb("ones", [P, P])
        tri = sb("tri", [P, P])
        mask = sb("mask", [P, 2 * P])
        dg = sb("dg", [P, TT, P])
        par = sb("par", [P, P])
        bada = sb("bada", [P, 9 * KD])
        cond = sb("cond", [P, KD])
        mod = sb("mod", [P, 9 * KD])
        m_st = sb("m_st", [P, 16, 4])
        h_sq = sb("h_sq", [P, 4, TT, MH])
        ss4 = sb("ss4", [P, TT, 4])
        gain = sb("gain", [P, KD])
        st = sb("st", [P, 8, 2])
        sink_row = sb("sink_row", [P, HQ])
        gb_row = sb("gb_row", [P, 2, MH])
        inv_f = sb("inv_f", [P, HALF])
        pos_i = sb("pos_i", [P, TT], I32)
        ang = sb("ang", [P, 8, TT, HALF])
        with ExitStack() as inner:
            hid_hi = inner.enter_context(nc.sbuf_tensor("hid_hi", [P, KD, T], F32R))
            hid_lo = inner.enter_context(nc.sbuf_tensor("hid_lo", [P, KD, T], F32R))
            pad = inner.enter_context(nc.sbuf_tensor("pad", [P, 1024], F32))
            gt_row = inner.enter_context(nc.sbuf_tensor("gt_row", [P, D], F32))
            fin_row = inner.enter_context(nc.sbuf_tensor("fin_row", [P, D], F32))
        proj = sb("proj", [P, TT, OG])
        gates = sb("gates", [P, TT, 2 * D])

        pa = psum("pa", [P, TT, NC])
        pb = psum("pb", [P, TT, NC])
        px = psum("px", [P, 2, NC])
        pm = psum("pm", [P, NC])
        pr = psum("pr", [P, NC])

        params_in = sem("params_in")
        rows_in = sem("rows_in")
        x_in = sem("x_in")
        fin_in = sem("fin_in")
        raw_in = [sem(f"raw_in{r}") for r in range(RING)]
        ada_in = [sem(f"ada_in{r}") for r in range(ADA_RING)]
        consts = sem("consts")
        par_tr = sem("par_tr")
        par_ok = sem("par_ok")
        cond_ok = sem("cond_ok")
        hi_done = sem("hi_done")
        lo_done = sem("lo_done")
        unit_used = sem("unit_used")
        ada_done = sem("ada_done")
        flushed = sem("flushed")
        mod_ok = sem("mod_ok")
        pa_free = sem("pa_free")
        pb_free = sem("pb_free")
        nat_ok = sem("nat_ok")
        nat_tr = sem("nat_tr")
        nat_hi = sem("nat_hi")
        nat_lo = sem("nat_lo")
        gt_diag = sem("gt_diag")
        gt_mm = sem("gt_mm")
        gt_ok = sem("gt_ok")
        h_ok = sem("h_ok")
        ss_ok = sem("ss_ok")
        rt_ok = sem("rt_ok")
        diag_ok = sem("diag_ok")
        gain_ok = sem("gain_ok")
        rms_row = sem("rms_row")
        xt_mm = sem("xt_mm")
        xt_f = sem("xt_f")
        xt_hi = sem("xt_hi")
        xt_lo = sem("xt_lo")
        dve_step = sem("dve_step")
        act_step = sem("act_step")
        proj_ok = sem("proj_ok")
        rope_ang = sem("rope_ang")
        trig_ok = sem("trig_ok")
        rope_ok = sem("rope_ok")
        kt_mm = sem("kt_mm")
        kt_ok = sem("kt_ok")
        q_in = sem("q_in")
        q_mm = sem("q_mm")
        q_ok = sem("q_ok")
        sc_mm = sem("sc_mm")
        mx_ok = sem("mx_ok")
        p_ok = sem("p_ok")
        pt_mm = sem("pt_mm")
        pt_ok = sem("pt_ok")
        o_mm = sem("o_mm")
        o_ok = sem("o_ok")
        g_abs = sem("g_abs")
        g_ln = sem("g_ln")
        g_logf = sem("g_logf")
        g_cum = sem("g_cum")
        g_diag = sem("g_diag")
        g_row = sem("g_row")
        g_rowok = sem("g_rowok")
        m_tr = sem("m_tr")
        m_pad = sem("m_pad")
        m_conv = sem("m_conv")
        m_qk = sem("m_qk")
        m_sc = sem("m_sc")
        m_max = sem("m_max")
        m_q = sem("m_q")
        ada_zero = sem("ada_zero")
        bada_ok = sem("bada_ok")
        gate_sig = sem("gate_sig")
        m_w = sem("m_w")
        m_a = sem("m_a")
        m_at = sem("m_at")
        m_atok = sem("m_atok")
        m_num = sem("m_num")
        m_h = sem("m_h")
        m_ss = sem("m_ss")
        m_var = sem("m_var")
        m_rt = sem("m_rt")
        m_out = sem("m_out")
        fin_ok = sem("fin_ok")
        stored = sem("stored")

        PAR = {}
        par_rows = []
        for name, src, n in (("g1", norm1_g.rearrange("a (k p) -> (a k) p", p=P), KD),
                             ("g2", norm2_g.rearrange("a (k p) -> (a k) p", p=P), KD),
                             ("g3", norm3_g.rearrange("a (k p) -> (a k) p", p=P), KD),
                             ("conv_w", conv_w.rearrange("a j (k p) -> (a j k) p", p=P), CONV * MQK2 // P),
                             ("conv_b", conv_b.rearrange("a (k p) -> (a k) p", p=P), MQK2 // P),
                             ("c", c.rearrange("a (k p) -> (a k) p", p=P), KD),
                             ("mg", mlstm_norm_g.rearrange("a (k p) -> (a k) p", p=P), MW // P)):
            PAR[name] = len(par_rows) and sum(r[1] for r in par_rows)
            par_rows.append((src, n, PAR[name]))
        NPAR = sum(r[1] for r in par_rows)
        assert NPAR <= P
        bada_rows = b_ada.rearrange("a (k p) -> (a k) p", p=P)
        NB = 9 * KD
        x_tok = x.rearrange("a (t p) d -> (a p) t d", p=P)
        out_tok = out.rearrange("a (t p) d -> (a p) t d", p=P)
        wada = w_ada.rearrange("a (k p) n -> p (a k) n", p=P)
        w_ffn_in = {1: ffn1_w_in.rearrange("a (k p) n -> p (a k) n", p=P),
                    2: ffn2_w_in.rearrange("a (k p) n -> p (a k) n", p=P)}
        w_ffn_out = {1: ffn1_w_out.rearrange("a (k p) n -> p (a k) n", p=P),
                     2: ffn2_w_out.rearrange("a (k p) n -> p (a k) n", p=P)}
        w_in_k = w_in.rearrange("a (k p) n -> p (a k) n", p=P)
        w_att_k = w_att_up.rearrange("a (k p) n -> p (a k) n", p=P)
        w_m_k = w_mlstm_up.rearrange("a (k p) n -> p (a k) n", p=P)
        w_out_k = w_out.rearrange("a (k p) n -> p (a k) n", p=P)

        def over(eng, n, body):
            body(0, True)
            if n > 1:
                with eng.Fori(1, n) as i:
                    body(i, False)

        block = ctx.enter_context(nc.Block())

        @block.sync
        def _(sp):
            for src, n, row in par_rows:
                sp.dma_start(par_in[row:row + n, :], src).then_inc(params_in, 16)
            sp.dma_start(bada_in[:, 0, :], bada_rows[0:P, :]).then_inc(params_in, 16)
            sp.dma_start(bada_in[0:NB - P, 1, :], bada_rows[P:NB, :]).then_inc(params_in, 16)

            def load_ada(name, i, j):
                what = ada_tile(name, i, j)
                if what is None:
                    return
                tile, half_row, kt = what
                if not (isinstance(tile, int) and tile < ADA_RING):
                    sp.wait_ge(ada_done, tile - (ADA_RING - 1))
                sp.dma_start(ada_w[:, j % ADA_RING, :],
                             wada[:, bass.ds(kt, 1), ROW[half_row] * ADA_W:(ROW[half_row] + 1) * ADA_W])\
                    .then_inc(ada_in[j % ADA_RING], 16)

            def load(ph, i, j, src, kn, w=NC):
                cidx = ph.c0 + ph.per * i + j
                if not (isinstance(cidx, int) and cidx < RING):
                    sp.wait_ge(unit_used, 2 * (cidx - (RING - 1)))
                sp.dma_start(raw[:, j % RING, 0:kn, 0:w], src).then_inc(raw_in[j % RING], 16)

            def ffn_chunk(name, i, g, pos, j):
                src = w_ffn_in[int(name[3])][:, (j % 4) * 4:(j % 4) * 4 + 4, bass.ds(g * NC + (j // 4) * FF, NC)]
                load(plan[name], i, pos, src, 4)

            sp.dma_start(pos_i[:, :], positions.rearrange("a (t p) -> (a p) t", p=P),
                         allow_slow_non_contiguous=True).then_inc(rows_in, 16)
            sp.dma_start(sink_row[:, :], sinks.broadcast_to([P, HQ])).then_inc(rows_in, 16)
            sp.dma_start(gb_row[:, 0, :], b_igate.broadcast_to([P, MH])).then_inc(rows_in, 16)
            sp.dma_start(gb_row[:, 1, :], b_fgate.broadcast_to([P, MH])).then_inc(rows_in, 16)
            sp.dma_start(h[:, :, :], x_tok).then_inc(x_in, 16)
            over(sp, 4, lambda i, first: [load_ada("start0", i, j) for j in range(8)])
            for pos in range(4):
                ffn_chunk("ffn1_in0", 0, 0, pos, FIRST_CHUNKS[pos])
            over(sp, 4, lambda i, first: [load_ada("start1", i, j) for j in range(8)])

            def load_ffn(f):
                g0 = 0
                for p, ng in enumerate(PARTS):
                    name = f"ffn{f}_in{p}"
                    def ffn_in(i, first, name=name, g0=g0):
                        for j in range(8):
                            if first and name == "ffn1_in0":
                                if j >= 4:
                                    ffn_chunk(name, 0, 0, j, FIRST_CHUNKS[j])
                                    for tile in FIRST_TILES.get(j, ()):
                                        load_ada(name, 0, tile)
                                continue
                            ffn_chunk(name, i, i + g0, j, j)
                            if name in ADA:
                                load_ada(name, i, j)
                    over(sp, ng, ffn_in)
                    name = f"ffn{f}_out{p}"
                    def ffn_out(b, first, name=name, g0=g0, ng=ng):
                        for j in range(4):
                            src = w_ffn_out[f][:, g0 * 4 + j * ng:g0 * 4 + (j + 1) * ng, bass.ds(b * NC, NC)]
                            load(plan[name], b, j, src, ng)
                            if name in ADA:
                                load_ada(name, b, j)
                    over(sp, 4, ffn_out)
                    g0 += ng

            load_ffn(1)

            def proj_pair(name, col0):
                def body(i, first):
                    for j in range(8):
                        src = w_in_k[:, (j % 4) * 4:(j % 4) * 4 + 4,
                                     bass.ds(i * (2 * NC) + (col0 + (j // 4) * NC), NC)]
                        load(plan[name], i, j, src, 4)
                        if name in ADA:
                            load_ada(name, i, j)
                over(sp, 4, body)

            proj_pair("proj", 0)
            for j in range(4):
                load(plan["rest"], 0, j, w_in_k[:, j * 4:j * 4 + 4, 8 * NC:OG], 4, REST_W)
            proj_pair("gates", OG)

            def up(i, first):
                for j in range(4):
                    w = w_att_k if j < 2 else w_m_k
                    load(plan["up"], i, j, w[:, (j % 2) * 4:(j % 2) * 4 + 4, bass.ds(i * NC, NC)], 4)
                    if not first:
                        load_ada("up", i, j)
                    elif j == 1:
                        sp.wait_ge(o_ok, HQ // 2)
                        sp.wait_ge(m_num, MH)
                        for tile in range(4):
                            load_ada("up", i, tile)
            over(sp, 4, up)

            def wout(i, first):
                for j in range(4):
                    load(plan["wout"], i, j, w_out_k[:, j * 4:j * 4 + 4, bass.ds(i * NC, NC)], 4)
                    load_ada("wout", i, j)
            over(sp, 4, wout)
            sp.wait_ge(nat_ok, plan["up"].nat0 + 4)
            sp.dma_start(fin_row[:, :], final_g.rearrange("(a d) -> a d", a=1).broadcast_to([P, D]))\
                .then_inc(fin_in, 16)
            load_ffn(2)
            for q in range(4):
                sp.wait_ge(fin_ok, q + 1)
                cols = slice((q % 2) * (D // 2), (q % 2 + 1) * (D // 2))
                sp.dma_start(out_tok[:, q // 2, cols], h[:, q // 2, cols]).then_inc(stored, 16)
            sp.wait_ge(stored, 64)

        @block.gpsimd
        def _(pool):
            pool.memset(ident[:, :], 0.0)
            pool.memset(ones[:, :], 1.0)
            pool.memset(tri[:, :], 1.0)
            pool.memset(mask[:, :], 0.0).then_inc(consts, 1)
            pool.wait_ge(consts, 1)
            pool.affine_select(out=ident[:, :], in_=ident[:, :], compare_op=ALU.not_equal, fill=1.0,
                               base=0, pattern=[[-1, P]], channel_multiplier=1)
            pool.affine_select(out=tri[:, :], in_=tri[:, :], compare_op=ALU.is_ge, fill=0.0,
                               base=0, pattern=[[1, P]], channel_multiplier=-1)
            pool.affine_select(out=mask[:, P:2 * P], in_=mask[:, P:2 * P], compare_op=ALU.is_ge, fill=NEG,
                               base=0, pattern=[[-1, P]], channel_multiplier=1)
            pool.affine_select(out=mask[:, 0:P], in_=mask[:, 0:P], compare_op=ALU.is_ge, fill=NEG,
                               base=-1, pattern=[[1, P]], channel_multiplier=-1).then_inc(consts, 1)

        def m_cols(hd, qk):
            cs = OM + qk * (MQK2 // 2) + hd * DK
            return proj[:, :, cs:cs + DK]

        def units(chunks, kn):
            for j in range(chunks):
                for half in (0, 1):
                    n = min(2, kn - 2 * half)
                    yield j, half, j * kn + 2 * half, n

        @block.tensor
        def _(pe):
            def unit(ph, i, j, half, k0, n, a_hi, a_lo, bank, start, stop, w=NC):
                u = 2 * (ph.c0 + ph.per * i + j) + half
                pe.wait_ge(lo_done, u + 1)
                for kk in range(n):
                    w_hi = hi[:, (2 * j + half) % 4, kk, 0:w]
                    w_lo = lo[:, j % RING, 2 * half + kk, 0:w]
                    for tt in range(TT):
                        tok = slice(tt * P, (tt + 1) * P)
                        ps = bank[:, tt, 0:w]
                        pe.matmul(ps, a_hi[:, k0 + kk, tok], w_hi, start=start and kk == 0, stop=False)
                        pe.matmul(ps, a_hi[:, k0 + kk, tok], w_lo, start=False, stop=False)
                        mm = pe.matmul(ps, a_lo[:, k0 + kk, tok], w_hi, start=False,
                                       stop=stop and kk == n - 1)
                mm.then_inc(unit_used, 1)

            def transposes(nb):
                pe.wait_ge(nat_ok, nb + 1)
                for b in (0, 1):
                    for ft in (0, 1):
                        for tt in range(TT):
                            mm = pe.transpose(px[:, b, ft * T + tt * P:ft * T + (tt + 1) * P],
                                              buf_b[:, tt, (2 * b + ft) * P:(2 * b + ft + 1) * P], ident[:, :])
                    mm.then_inc(nat_tr, 1)

            def flush(half_row):
                e = flush_no(half_row)
                first, halves = flush_at[e]
                pe.wait_ge(ada_done, tiles_of[e])
                if e > 0:
                    pe.wait_ge(mod_ok, e)
                if first > 2 * GT1 + 1:
                    pe.wait_ge(gt_ok, 8 if first > 14 else 4)
                for s in range(8 * halves):
                    mm = pe.matmul(pm[:, s:s + 1], ada_acc[:, (first + s // 8) % 2, (s % 8) * P:(s % 8 + 1) * P],
                                   ones[:, 0:1], start=True, stop=True)
                mm.then_inc(flushed, 1)

            def gate_rows(n):
                pe.wait_ge(gt_diag, n + 1)
                for q in range(4):
                    if q >= 2:
                        pe.wait_ge(gt_ok, 4 * n + q - 1)
                    pe.matmul((pr, pm)[q % 2][:, :], ones[:, :], gt_row[:, q * NC:(q + 1) * NC],
                              start=True, stop=True).then_inc(gt_mm, 1)

            def in_body(ph, i, first, nat, turn_group=None, g0=0, step=None):
                if turn_group:
                    turn_group(0)
                    turn_group(1)
                if not (isinstance(i, int) and i + ph.a0 == 0):
                    pe.wait_ge(pa_free, ph.a0 + i)
                for n_, (j, half, k0, n) in enumerate(units(8, 4)):
                    if n_ == 8:
                        if nat and not first:
                            transposes(ph.nat0 + i - 1)
                        if not nat:
                            pe.wait_ge(pb_free, ph.b0 + i)
                        elif first and ph.b0 > 0:
                            pe.wait_ge(pb_free, ph.b0)
                    if step:
                        step(n_)
                    if turn_group and n_ < 8:
                        pe.wait_ge(xt_lo, g0 + n_ + 1)
                    unit(ph, i, j, half, k0 % KD, n, act_hi, act_lo, pa if n_ < 8 else pb, n_ % 8 == 0, n_ % 8 == 7)
                    if turn_group and n_ < 6:
                        turn_group(n_ + 2)

            def out_phase(ph, kn, nat_last, gate=None):
                for b in range(4):
                    bank, free, use0 = (pa, pa_free, ph.a0) if b % 2 == 0 else (pb, pb_free, ph.b0)
                    if b == 1 and gate is not None:
                        gate_rows(gate)
                    pe.wait_ge(free, use0 + b // 2)
                    for j, half, k0, n in units(4, kn):
                        if b == 0 and k0 < 4 * (kn - 1) < k0 + n + 1 or (b == 0 and k0 == 4 * (kn - 1)):
                            pe.wait_ge(nat_lo, 2 * (nat_last + 1))
                        unit(ph, b, j, half, k0, n, hid_hi, hid_lo, bank, (j, half) == (0, 0),
                             k0 + n == 4 * kn)
                        if b == 0 and (j, half) == (1, 1):
                            transposes(nat_last)

            def turn(g, count, src, scaled=False):
                if count >= 2:
                    pe.wait_ge(xt_f, count - 1)
                for k in (0, 1):
                    for tt in range(TT):
                        dst = px[:, g % 2, k * T + tt * P:k * T + (tt + 1) * P]
                        if scaled:
                            mm = pe.matmul(dst, src(tt, 2 * g + k), dg[:, tt, :], start=True, stop=True)
                        else:
                            mm = pe.transpose(dst, src(tt, 2 * g + k), ident[:, :])
                mm.then_inc(xt_mm, 1)

            def norm_group(n, g):
                def src(tt, k):
                    return h[:, tt, k * P:(k + 1) * P]

                if n == 0:
                    if g == 0:
                        pe.wait_ge(diag_ok, 1)
                    turn(g, g, src, scaled=True)
                    return
                if g == 0:
                    pe.wait_ge(h_ok, (0, 9, 13)[n])
                if g == 2:
                    pe.wait_ge(h_ok, (0, 12, 16)[n])
                turn(g, (0, 8, 24)[n] + g, src)
                if g == 1:
                    pe.wait_ge(diag_ok, n + 1)
                    pe.wait_ge(gt_ok, 4 * n)
                    pe.matmul(pr[:, 0:T], ones[:, :], dg[:, :, :].rearrange("p a b -> p (a b)"),
                              start=True, stop=True).then_inc(rms_row, 1)

            def first_body(ph):
                norm_group(0, 0)
                norm_group(0, 1)
                for n_ in range(16):
                    j, half = FIRST_CHUNKS[n_ // 2], n_ % 2
                    g = 2 * (j % 4) + half
                    if n_ == 8:
                        flush(2)
                        pe.wait_ge(gain_ok, 1)
                        norm_group(0, 4)
                        norm_group(0, 5)
                    pe.wait_ge(xt_lo, g + 1)
                    unit(ph, 0, n_ // 2, half, 2 * g, 2, act_hi, act_lo, pa if j < 4 else pb, g == 0, g == 7)
                    if n_ in (0, 1, 8, 9):
                        norm_group(0, (2, 3, 6, 7)[n_ % 8 + 2 * (n_ // 8)])

            def ffn(f):
                for p, ng in enumerate(PARTS):
                    name = f"ffn{f}_in{p}"
                    ph = plan[name]
                    n = 0 if f == 1 else 2
                    if name == "ffn1_in1":
                        flush(6)
                    if name == "ffn1_in2":
                        flush(9)
                    if name == "ffn2_in0":
                        flush(15)

                    def body(i, first):
                        if first and name == "ffn1_in0":
                            first_body(ph)
                            return
                        in_body(ph, i, first, True, turn_group=(lambda g: norm_group(n, g)) if first and p == 0 else None,
                                g0=(0, 8, 24)[n])
                    over(pe, ng, body)
                    name = f"ffn{f}_out{p}"
                    done = {"ffn1_out0": 4, "ffn1_out1": 7, "ffn1_out2": 10, "ffn2_out0": 16}.get(name)
                    if done is not None:
                        flush(done)
                    out_phase(plan[name], ng, ph.nat0 + ng - 1, gate={"ffn1_out0": 0, "ffn2_out0": 2}.get(name))

            pe.wait_ge(consts, 2)
            pe.wait_ge(params_in, 16 * (len(par_rows) + 2))
            pe.transpose(px[:, 0, 0:NPAR], par_in[0:NPAR, :], ident[0:NPAR, 0:NPAR])
            pe.transpose(px[:, 0, P:2 * P], bada_in[:, 0, :], ident[:, :])
            pe.transpose(px[:, 0, 2 * P:P + NB], bada_in[0:NB - P, 1, :], ident[0:NB - P, 0:NB - P])\
                .then_inc(par_tr, 1)
            pe.wait_ge(par_ok, 1)
            pe.wait_ge(bada_ok, 1)
            flush(0)
            ffn(1)
            flush(11)
            ph = plan["proj"]

            def proj_step(n_):
                if n_ == 6:
                    pe.wait_ge(rope_ok, 1)
                    for g in range(KV):
                        for tt in range(TT):
                            mm = pe.transpose(pr[0:HD, g * T + tt * P:g * T + (tt + 1) * P],
                                              proj[:, tt, OK + g * HD:OK + (g + 1) * HD], ident[:, :])
                    mm.then_inc(kt_mm, 1)
                if n_ in (5, 7, 9, 11):
                    hd = (n_ - 5) // 2
                    pe.wait_ge(pa_free, ph.a0 + 3)
                    pe.wait_ge(pb_free, ph.b0 + 2)
                    if hd >= 2:
                        pe.wait_ge(m_pad, hd - 1)
                    for qk in (0, 1):
                        for tt in range(TT):
                            cs = OM + qk * (MQK2 // 2) + hd * DK
                            mm = pe.transpose(px[:, hd % 2, qk * T + tt * P:qk * T + (tt + 1) * P],
                                              proj[:, tt, cs:cs + DK], ident[:, :])
                    mm.then_inc(m_tr, 1)

            over(pe, 3, lambda i, first: in_body(ph, i, first, False, g0=8,
                                                 turn_group=(lambda g: norm_group(1, g)) if first else None))
            in_body(ph, 3, False, False, step=proj_step)
            flush(12)
            ph = plan["rest"]
            pe.wait_ge(pa_free, ph.a0)
            for n_, (j, half, k0, n) in enumerate(units(4, 4)):
                unit(ph, 0, j, half, k0, n, act_hi, act_lo, pa, n_ == 0, n_ == 7, REST_W)
                if n_ == 3:
                    pe.wait_ge(g_logf, 1)
                    pe.matmul(pm[:, 0:MH], tri[:, :], m_st[:, 0, :], start=True, stop=True)
                    pe.matmul(pm[:, MH:2 * MH], tri[:, :], m_st[:, 1, :], start=True, stop=False)
                    pe.matmul(pm[:, MH:2 * MH], ones[:, :], m_st[:, 0, :], start=False, stop=True)\
                        .then_inc(g_cum, 1)
                if n_ == 7:
                    pe.wait_ge(g_diag, 1)
                    pe.wait_ge(kt_ok, 1)
                    for tt in range(TT):
                        mm = pe.matmul((pr, pm)[tt][:, :], ones[:, :], dgm[:, tt, :, :].rearrange("p a b -> p (a b)"),
                                       start=True, stop=True)
                    mm.then_inc(g_row, 1)

            def q_turn(n):
                pe.wait_ge(q_in, n + 1)
                for tt in range(TT):
                    mm = pe.transpose(px[:, 0, tt * P:(tt + 1) * P], q_st[:, tt, :], ident[:, :])
                mm.then_inc(q_mm, 1)

            def scores(n):
                pe.wait_ge(q_ok, n + 1)
                if not (isinstance(n, int) and n == 0):
                    pe.wait_ge(o_ok, n)
                for hh in (0, 1):
                    pe.matmul(pm[:, hh * P:(hh + 1) * P], q_t[:, hh, 0:P], k_g[:, 0:P], start=True, stop=True)
                    mm = pe.matmul(pr[:, hh * T:(hh + 1) * T], q_t[:, hh, P:T], k_g[:, :], start=True, stop=True)
                mm.then_inc(sc_mm, 1)

            def p_turn(n):
                pe.wait_ge(p_ok, n + 1)
                for hh in (0, 1):
                    for b in range(3):
                        mm = pe.transpose(px[:, hh, b * P:(b + 1) * P], s_sb[:, hh, b * P:(b + 1) * P], ident[:, :])
                mm.then_inc(pt_mm, 1)

            def values(n, g):
                pe.wait_ge(pt_ok, n + 1)
                for hh in (0, 1):
                    v0, v1 = (proj[:, tt, bass.ds(g * HD + OV, HD)] for tt in range(TT))
                    pe.matmul(pm[:, hh * HD:(hh + 1) * HD], p_t[:, hh, 0, :], v0, start=True, stop=True)
                    dst = pm[:, (2 + hh) * HD:(3 + hh) * HD]
                    pe.matmul(dst, p_t[:, hh, 1, :], v0, start=True, stop=False)
                    mm = pe.matmul(dst, p_t[:, hh, 2, :], v1, start=False, stop=True)
                mm.then_inc(o_mm, 1)

            def heads_step(i, n_):
                g = i // 2
                if n_ == 0:
                    pe.wait_ge(m_pad, MH)
                    q_turn(2 * i)
                if n_ == 1:
                    pe.wait_ge(m_q, i + 1)
                    pe.matmul(px[:, 1, 0:P], mq_t[:, 0, 0:P], mq_t[:, 1, 0:P], start=True, stop=True)
                    pe.matmul(px[:, 1, P:3 * P], mq_t[:, 0, P:T], mq_t[:, 1, :], start=True, stop=True)\
                        .then_inc(m_sc, 1)
                if n_ == 2:
                    pe.wait_ge(g_rowok, 1)
                    scores(2 * i)
                if n_ == 4:
                    pe.wait_ge(m_a, i + 1)
                    pe.wait_ge(mx_ok, 2 * i + 1)
                    for b in range(3):
                        mm = pe.transpose(pr[:, b * P:(b + 1) * P], w_sb[:, b * P:(b + 1) * P], ident[:, :])
                    mm.then_inc(m_at, 1)
                if n_ == 5:
                    p_turn(2 * i)
                if n_ == 7:
                    values(2 * i, g)
                    q_turn(2 * i + 1)
                if n_ == 8:
                    pe.wait_ge(m_atok, i + 1)
                    v0, v1 = (proj[:, tt, bass.ds(i * MV + OMV, MV)] for tt in range(TT))
                    pe.matmul(pr[:, 0:MV], a_t[:, 0, :], v0, start=True, stop=True)
                    pe.matmul(pr[:, MV:2 * MV], a_t[:, 1, :], v0, start=True, stop=False)
                    pe.matmul(pr[:, MV:2 * MV], a_t[:, 2, :], v1, start=False, stop=True).then_inc(m_num, 1)
                if n_ == 10:
                    pe.wait_ge(m_h, i + 1)
                    scores(2 * i + 1)
                if n_ == 13:
                    p_turn(2 * i + 1)
                if n_ == 15:
                    values(2 * i + 1, g)

            over(pe, 4, lambda i, first: in_body(plan["gates"], i, first, False, step=lambda n_: heads_step(i, n_)))

            ph = plan["up"]

            def out_group(g):
                if g == 4:
                    pe.wait_ge(m_out, MH)
                if g == 0:
                    pe.wait_ge(o_ok, HQ // 2)
                turn(g, 16 + g, lambda tt, k: proj[:, tt, k * P:(k + 1) * P] if k < 8
                     else proj[:, tt, OMV + (k - 8) * P:OMV + (k - 7) * P])

            def up(i, first):
                if first:
                    out_group(0)
                    out_group(1)
                for n_, (j, half, k0, n) in enumerate(units(4, 4)):
                    if n_ == 0:
                        pe.wait_ge(pa_free, ph.a0 + i)
                    if n_ == 4:
                        if not first:
                            transposes(ph.nat0 + i - 1)
                        pe.wait_ge(pb_free, ph.b0 + i)
                    if first:
                        pe.wait_ge(xt_lo, 16 + n_ + 1)
                    unit(ph, i, j, half, k0, n, act_hi, act_lo, pa if n_ < 4 else pb, n_ % 4 == 0, n_ % 4 == 3)
                    if first and n_ < 6:
                        out_group(n_ + 2)
            over(pe, 4, up)
            flush(14)
            out_phase(plan["wout"], 4, ph.nat0 + 3, gate=1)
            ffn(2)

        @block.scalar
        def _(act):
            steps = [0]

            def link(ins):
                steps[0] += 1
                ins.then_inc(act_step, 1)
                act.wait_ge(act_step, steps[0])

            def split(ph, i, j, half, n, w=NC):
                u = 2 * (ph.c0 + ph.per * i + j) + half
                if half == 0:
                    act.wait_ge(raw_in[j % RING], 16 * (ph.c0 // RING + (ph.per // RING) * i + j // RING + 1))
                if not (isinstance(u, int) and u < 4):
                    act.wait_ge(unit_used, u - 3)
                act.copy(hi[:, (2 * j + half) % 4, 0:n, 0:w], raw[:, j % RING, 2 * half:2 * half + n, 0:w])\
                    .then_inc(hi_done, 1)

            def nat_evac_at(nb, slot):
                for b in (0, 1):
                    act.wait_ge(consts, 2)
                    act.wait_ge(nat_tr, 2 * nb + b + 1)
                    k = 4 * slot + 2 * b
                    act.copy(hid_hi[:, bass.ds(k, 2), :], px[:, b, :].rearrange("p (k t) -> p k t", k=2))\
                        .then_inc(nat_hi, 1)

            def in_body(ph, i, first, evac_a, evac_b, nat, mid=None, step=None):
                for n_, (j, half, k0, n) in enumerate(units(8, 4)):
                    split(ph, i, j, half, n)
                    if first and mid:
                        mid(n_)
                    if n_ == 3 and not first and evac_b:
                        evac_b(i - 1)
                    if n_ == (15 if first and ph.c0 == 0 else 11):
                        evac_a(i)
                        if nat and not first:
                            nat_evac_at(ph.nat0 + i - 1, i - 1)
                    if step:
                        step(n_)

            def squares(h_blocks, b):
                act.wait_ge(h_ok, h_blocks)
                for tt in range(TT):
                    ins = act.activation(buf_b[:, tt, :], h[:, tt, b * NC:(b + 1) * NC], ACT.Square,
                                         accum_out=ss4[:, tt, b:b + 1])
                ins.then_inc(ss_ok, 1)

            def out_phase(ph, kn, nat_last, gate=None, scale=1.0, sq=None):
                for b in range(4):
                    for n_, (j, half, k0, n) in enumerate(units(4, kn)):
                        split(ph, b, j, half, n)
                        if b == 0 and n_ == 7:
                            nat_evac_at(nat_last, kn - 1)
                        if b == 1 and n_ == 3 and gate is not None:
                            for q in range(4):
                                act.wait_ge(gt_mm, 4 * gate + q + 1)
                                act.activation(gt_row[:, q * NC:(q + 1) * NC], (pr, pm)[q % 2][:, :],
                                               ACT.Copy, scale=scale).then_inc(gt_ok, 1)
                        if b > 0 and n_ == 5 and sq is not None:
                            squares(sq + b, b - 1)

            def turn_affine(g, count, scale, bias):
                act.wait_ge(xt_mm, count + 1)
                if count >= 2:
                    act.wait_ge(xt_lo, count - 1)
                if scale is None:
                    act.copy(buf_a[:, g % 2, :], px[:, g % 2, :]).then_inc(xt_f, 1)
                    return
                for k in (0, 1):
                    kt = 2 * g + k
                    ins = act.activation(buf_a[:, g % 2, k * T:(k + 1) * T], px[:, g % 2, k * T:(k + 1) * T],
                                         ACT.Identity, scale=scale(kt), bias=bias(kt))
                ins.then_inc(xt_f, 1)

            def root_table():
                act.activation(st[:, 2, :], ones[:, 0:TT], ACT.Sqrt)

            def root(n):
                act.wait_ge(rt_ok, 2 * n + 1)
                act.activation(st[:, 2, :], st[:, 1, :], ACT.Sqrt).then_inc(rt_ok, 1)

            def norm(n, h_blocks, sh, g0, n_):
                if n_ == (3 if n > 0 else 0):
                    if n > 0:
                        root_table()
                        squares(h_blocks, 3)
                        root(n)
                    act.wait_ge(diag_ok, n + 1)
                for g in (FIRST_AT if n == 0 else GROUPS_AT).get(n_, ()):
                    if (n, g) == (0, 4):
                        act.wait_ge(gain_ok, 1)
                    turn_affine(g, g0 + g, lambda k: gain[:, k:k + 1],
                                lambda k: mod[:, sh * KD + k:sh * KD + k + 1] if n == 0 else 0.0)

            def silu(k):
                def run(i):
                    first = isinstance(i, int) and k.nat0 + i == 0
                    act.wait_ge(unit_used, 2 * (k.c0 + k.per * i) + (12 if first else 8))
                    if not (isinstance(i, int) and k.nat0 + i == 0):
                        act.wait_ge(nat_ok, k.nat0 + i)
                    act.activation(buf_a[:, :, :], pa[:, :, :], ACT.Silu).then_inc(pa_free, 1)
                return run

            def ffn(f, mid):
                for p, ng in enumerate(PARTS):
                    ph = plan[f"ffn{f}_in{p}"]
                    over(act, ng, lambda i, first: in_body(ph, i, first, silu(ph), None, True,
                                                           mid=mid if p == 0 else None))
                    name = f"ffn{f}_out{p}"
                    out_phase(plan[name], ng, ph.nat0 + ng - 1,
                              gate={"ffn1_out0": 0, "ffn2_out0": 2}.get(name), scale=0.5,
                              sq=(8 if f == 1 else 24) if p == 2 else None)

            act.wait_ge(par_ok, 1)
            act.activation(cond[:, :], par[:, PAR["c"]:PAR["c"] + KD], ACT.Silu).then_inc(cond_ok, 1)
            act.wait_ge(rope_ang, 1)
            act.activation(ang[:, 6:8, :, :], ang[:, 4:6, :, :], ACT.Sin).then_inc(trig_ok, 1)
            act.wait_ge(x_in, 16)
            act.wait_ge(bada_ok, 1)
            for b in range(3):
                for tt in range(TT):
                    ins = act.activation(buf_b[:, tt, :], h[:, tt, b * NC:(b + 1) * NC], ACT.Square,
                                         accum_out=ss4[:, tt, b:b + 1])
                link(ins)

            for tt in range(TT):
                ins = act.activation(buf_b[:, tt, :], h[:, tt, 3 * NC:], ACT.Square, accum_out=ss4[:, tt, 3:4])
            ins.then_inc(ss_ok, 4)
            root(0)
            ffn(1, lambda n_: norm(0, None, SH1, 0, n_))

            def evac(ph, bank, free, after, dst, func, c0):
                def run(i):
                    act.wait_ge(consts, 2)
                    act.wait_ge(unit_used, 2 * (ph.c0 + ph.per * i) + after)
                    act.activation(dst[:, :, bass.ds(i * (2 * NC) + c0, NC)], bank[:, :, :], func)\
                        .then_inc(free, 1)
                return run
            ph = plan["proj"]
            copy_a = evac(ph, pa, pa_free, 8, proj, ACT.Copy, 0)
            copy_b = evac(ph, pb, pb_free, 16, proj, ACT.Copy, NC)

            def proj_step(n_):
                if n_ == 9:
                    act.wait_ge(kt_mm, 1)
                    act.copy(k_t[:, :, :], pr[0:HD, :].rearrange("p (g t) -> p g t", g=KV)).then_inc(kt_ok, 1)
                if n_ in (8, 10, 12, 14):
                    hd = (n_ - 8) // 2
                    act.wait_ge(m_tr, hd + 1)
                    if hd > 0:
                        act.wait_ge(m_conv, hd)
                    act.copy(xpad[:, :, CONV - 1:], px[:, hd % 2, :].rearrange("p (a t) -> p a t", a=2))\
                        .then_inc(m_pad, 1)
            over(act, 3, lambda i, first: in_body(ph, i, first, copy_a, copy_b, False,
                                                  mid=lambda n_: norm(1, 12, SH2, 8, n_)))
            in_body(ph, 3, False, copy_a, copy_b, False, step=proj_step)

            rp = plan["rest"]
            for n_, (j, half, k0, n) in enumerate(units(4, 4)):
                split(rp, 0, j, half, n, REST_W)
                if n_ == 1:
                    act.wait_ge(g_abs, 1)
                    link(act.activation(m_st[:, 10:12, :], m_st[:, 8:10, :], ACT.Exp, scale=-1.0))
                    act.activation(m_st[:, 8:10, :], m_st[:, 10:12, :], ACT.Ln, bias=1.0).then_inc(g_ln, 1)
                if n_ == 3:
                    copy_b(3)
                if n_ == 5:
                    act.wait_ge(m_conv, MH)
                    for hd in range(MH):
                        for qk in (0, 1):
                            cb = PAR["conv_b"] + qk * MH + hd
                            dst = m_cols(hd, qk)
                            ins = act.activation(dst, dst, ACT.Silu, bias=par[:, cb:cb + 1])
                    ins.then_inc(m_qk, 1)
            act.wait_ge(g_row, 1)
            act.copy(r_row[:, :, 0:P], pr[:, :].rearrange("p (a t) -> p a t", a=MH))
            act.copy(r_row[:, :, P:T], pm[:, :].rearrange("p (a t) -> p a t", a=MH)).then_inc(g_rowok, 1)

            gp = plan["gates"]

            def rest_evac(n_):
                if n_ != 0:
                    return
                act.wait_ge(unit_used, 2 * rp.c0 + 8)
                act.copy(proj[:, :, 8 * NC:OG], pa[:, :, 0:REST_W]).then_inc(pa_free, 1)

            def pair_in(n):
                act.wait_ge(rope_ok, 1)
                if not (isinstance(n, int) and n == 0):
                    act.wait_ge(q_mm, n)
                act.copy(q_st[:, :, :], proj[:, :, bass.ds(n * (2 * HD), 2 * HD)]).then_inc(q_in, 1)

            def pair_q(n, g):
                act.wait_ge(q_mm, n + 1)
                act.copy(q_t[:, 0, :], px[0:HD, 0, 0:T])
                act.copy(k_g[:, :], k_t[:, g, :])
                act.copy(q_t[:, 1, :], px[HD:2 * HD, 0, 0:T]).then_inc(q_ok, 1)

            def pair_exp(n):
                act.wait_ge(mx_ok, n + 1)
                act.activation(m_st[:, 6, :], m_st[:, 5, :], ACT.Exp)
                for hh in (0, 1):
                    for b, cols in ((0, slice(0, P)), (1, slice(P, 3 * P))):
                        o = 2 * b + hh
                        ins = act.activation(s_sb[:, hh, cols], s_sb[:, hh, cols], ACT.Exp,
                                             bias=m_st[:, 4, o:o + 1], accum_out=m_st[:, 7, o:o + 1])
                ins.then_inc(p_ok, 1)

            def pair_pt(n):
                act.wait_ge(pt_mm, n + 1)
                act.copy(p_t[:, :, :, :], px[:, :, 0:3 * P].rearrange("p a (b t) -> p a b t", b=3))\
                    .then_inc(pt_ok, 1)

            def heads_step(i, n_):
                if n_ == 0:
                    pair_in(2 * i)
                    act.wait_ge(m_qk, 1)
                    for qk in (0, 1):
                        src = proj[:, :, bass.ds(i * DK + (OM + qk * (MQK2 // 2)), DK)]
                        ins = act.copy(mq_t[:, qk, :].rearrange("p (t c) -> p t c", t=TT), src)
                    ins.then_inc(m_q, 1)
                if n_ == 3:
                    pair_q(2 * i, i // 2)
                if n_ == 4:
                    act.wait_ge(m_max, i + 1)
                    act.activation(w_sb[:, 0:P], w_sb[:, 0:P], ACT.Exp, bias=m_st[:, 12, 0:1])
                    act.activation(w_sb[:, P:3 * P], w_sb[:, P:3 * P], ACT.Exp, bias=m_st[:, 12, 1:2])
                    act.activation(m_st[:, 13, 0:2], m_st[:, 13, 2:4], ACT.Exp).then_inc(m_w, 1)
                if n_ == 5:
                    pair_in(2 * i + 1)
                if n_ == 6:
                    pair_exp(2 * i)
                if n_ == 7:
                    act.wait_ge(m_at, i + 1)
                    act.copy(a_t[:, :, :], pr[:, 0:3 * P].rearrange("p (b t) -> p b t", b=3)).then_inc(m_atok, 1)
                if n_ == 8:
                    pair_pt(2 * i)
                if n_ == 10:
                    pair_q(2 * i + 1, i // 2)
                if n_ == 12:
                    act.wait_ge(m_h, i + 1)
                    for tt in range(TT):
                        ins = act.activation((w_sb, s_sb[:, 0, :])[tt][:, 0:MV], proj[:, tt, bass.ds(i * MV + OMV, MV)],
                                             ACT.Square, accum_out=h_sq[:, 0, tt, bass.ds(i, 1)])
                    ins.then_inc(m_ss, 1)
                if n_ == 14:
                    pair_exp(2 * i + 1)
                if n_ == 15:
                    pair_pt(2 * i + 1)
            graw_a = evac(gp, pa, pa_free, 8, gates, ACT.Copy, 0)
            graw_b = evac(gp, pb, pb_free, 16, gates, ACT.Copy, NC)
            over(act, 4, lambda i, first: in_body(gp, i, first, graw_a, graw_b, False, mid=rest_evac,
                                                  step=lambda n_: heads_step(i, n_)))

            ph = plan["up"]

            def m_group(g):
                turn_affine(g, 16 + g, lambda k: par[:, PAR["mg"] + k - 8:PAR["mg"] + k - 7], lambda k: 0.0)

            def up(i, first):
                for n_, (j, half, k0, n) in enumerate(units(4, 4)):
                    split(ph, i, j, half, n)
                    if first and n_ == 2:
                        act.wait_ge(m_var, 1)
                        act.activation(h_sq[:, 2, :, :], h_sq[:, 1, :, :], ACT.Sqrt).then_inc(m_rt, 1)
                    if first:
                        for g in OUT_AT.get(n_, ()):
                            if g < 4:
                                turn_affine(g, 16 + g, None, None)
                            else:
                                m_group(g)
                    if first and n_ == 3:
                        act.activation(proj[:, :, OO:OG], proj[:, :, OO:OG], ACT.Sigmoid).then_inc(proj_ok, 1)
                        graw_b(3)
                    if n_ == (5 if first else 3):
                        if first:
                            act.wait_ge(pa_free, gp.a0 + 4)
                            act.wait_ge(pb_free, gp.b0 + 4)
                        for c0 in (0, D):
                            g_ = gates[:, :, bass.ds(i * NC + c0, NC)]
                            act.activation(g_, g_, ACT.Sigmoid).then_inc(gate_sig, 1)
                if not first:
                    nat_evac_at(ph.nat0 + i - 1, i - 1)
            over(act, 4, up)
            out_phase(plan["wout"], 4, ph.nat0 + 3, gate=1, sq=12)
            ffn(2, lambda n_: norm(2, 16, SH3, 24, n_))
            root_table()
            squares(28, 3)
            root(3)

        @block.vector
        def _(dve):
            steps = [0]

            def link(ins):
                steps[0] += 1
                ins.then_inc(dve_step, 1)
                dve.wait_ge(dve_step, steps[0])

            def split(ph, i, j, half, n, w=NC):
                u = 2 * (ph.c0 + ph.per * i + j) + half
                dve.wait_ge(hi_done, u + 1)
                s = slice(2 * half, 2 * half + n)
                dve.tensor_tensor(lo[:, j % RING, s, 0:w], raw[:, j % RING, s, 0:w],
                                  hi[:, (2 * j + half) % 4, 0:n, 0:w].bitcast(F32), ALU.subtract)\
                    .then_inc(lo_done, 1)

            def ada(name, i, j):
                what = ada_tile(name, i, j)
                kind = ADA[name][0]
                if what is None:
                    if j == 0:
                        dve.wait_ge(flushed, flush_no(ADA[name][1] - 2) + 1)
                        dve.memset(ada_acc[:, ADA[name][1] % 2, :], 0.0).then_inc(ada_zero, 1)
                    return
                tile, half_row, kt = what
                dve.wait_ge(ada_in[j % ADA_RING], 16 * ada_use(name, i, j))
                wt = ada_w[:, j % ADA_RING, :]
                acc = ada_acc[:, half_row % 2, :]
                if isinstance(kt, int) and kt == 0:
                    if half_row > 1:
                        dve.wait_ge(flushed, flush_no(half_row - 2) + 1)
                    dve.tensor_scalar(acc, wt, cond[:, 0:1], None, ALU.mult).then_inc(ada_done, 1)
                    return
                dve.wait_ge(ada_done, tile - 1 if kind == "pair" else tile)
                if kind == "late":
                    dve.wait_ge(ada_zero, 1)
                dve.scalar_tensor_tensor(out=acc, in0=wt, scalar=cond[:, bass.ds(kt, 1)], in1=acc,
                                         op0=ALU.mult, op1=ALU.add).then_inc(ada_done, 1)

            def ada_use(name, i, j):
                tiles = 4 if ADA[name][0] == "one" else 8
                it = i - 1 if ADA[name][0] == "late" else i
                return ada_first[name] // ADA_RING + (tiles // ADA_RING) * it + j // ADA_RING + 1

            def norm_split(groups, n, sh, count0):
                for g in groups:
                    dve.wait_ge(xt_f, count0 + g + 1)
                    dve.wait_ge(rms_row, n)
                    t = buf_a[:, g % 2, :].rearrange("p (k t) -> p k t", k=2)
                    link(dve.tensor_tensor(t, t, pr[:, 0:T].unsqueeze(1).broadcast_to([P, 2, T]), ALU.mult))
                    shift = [mod[:, sh * KD + 2 * g + k:sh * KD + 2 * g + k + 1] for k in (0, 1)]
                    for k in (0, 1):
                        ins = dve.tensor_scalar(act_hi[:, 2 * g + k, :], t[:, k, :], shift[k], None, ALU.add)
                    ins.then_inc(xt_hi, 1)
                    dve.wait_ge(xt_hi, count0 + g + 1)
                    for k in (0, 1):
                        ins = dve.scalar_tensor_tensor(out=act_lo[:, 2 * g + k, :], in0=t[:, k, :], scalar=shift[k],
                                                       in1=act_hi[:, 2 * g + k, :].bitcast(F32),
                                                       op0=ALU.add, op1=ALU.subtract)
                    ins.then_inc(xt_lo, 1)

            def mod_row(half_row):
                e = flush_no(half_row)
                first, halves = flush_at[e]
                dve.wait_ge(flushed, e + 1)
                for k in range(halves):
                    row = ROW[first + k]
                    cols = slice(8 * row, 8 * (row + 1))
                    ins = dve.tensor_tensor(mod[:, cols], pm[:, 8 * k:8 * (k + 1)], bada[:, cols], ALU.add)
                ins.then_inc(mod_ok, 1)

            def nat_evac(nb, slot):
                for b in (0, 1):
                    dve.wait_ge(nat_hi, 2 * nb + b + 1)
                    k = 4 * slot + 2 * b
                    dve.tensor_tensor(hid_lo[:, bass.ds(k, 2), :], px[:, b, :].rearrange("p (k t) -> p k t", k=2),
                                      hid_hi[:, bass.ds(k, 2), :].bitcast(F32), ALU.subtract).then_inc(nat_lo, 1)

            def hidden(ph, i):
                dve.wait_ge(unit_used, 2 * (ph.c0 + ph.per * (i + 1)))
                dve.wait_ge(pa_free, ph.a0 + i + 1)
                dve.tensor_tensor(buf_b[:, :, :], buf_a[:, :, :], pb[:, :, :], ALU.mult)\
                    .then_inc(nat_ok, 1)

            def ffn_in(name, ng, mid):
                ph = plan[name]

                def body(i, first):
                    for n_, (j, half, k0, n) in enumerate(units(8, 4)):
                        split(ph, i, j, half, n)
                        if first and mid:
                            mid(n_)
                        if n_ == 3 and not first:
                            hidden(ph, i - 1)
                        if n_ == 11 and not first:
                            nat_evac(ph.nat0 + i - 1, i - 1)
                        if half == 1 and name in ADA:
                            if first and name == "ffn1_in0":
                                for tile in FIRST_TILES.get(j, ()):
                                    ada(name, 0, tile)
                            else:
                                ada(name, i, j)
                over(dve, ng, body)

            def add_out(ph, b, gate):
                bank, free = (pa, pa_free) if b % 2 == 0 else (pb, pb_free)
                dve.wait_ge(unit_used, 2 * (ph.c0 + ph.per * (b + 1)))
                if b == 0:
                    dve.wait_ge(gt_ok, 4 * gate + 4)
                row = gt_row[:, b * NC:(b + 1) * NC].unsqueeze(1).broadcast_to([P, TT, NC])
                dve.tensor_tensor(buf_a[:, :, :], bank[:, :, :], row, ALU.mult).then_inc(free, 1)
                use = (ph.a0 if b % 2 == 0 else ph.b0) + b // 2 + 1
                dve.wait_ge(free, use)
                hs = h[:, :, b * NC:(b + 1) * NC]
                dve.tensor_tensor(hs, hs, buf_a[:, :, :], ALU.add).then_inc(h_ok, 1)

            def out_phase(name, kn, nat_last, hid_tail, gate, flush_m=(), diag_m=None):
                ph = plan[name]
                for b in range(4):
                    for n_, (j, half, k0, n) in enumerate(units(4, kn)):
                        split(ph, b, j, half, n)
                        if n_ == 3:
                            if b == 0:
                                hid_tail()
                            else:
                                add_out(ph, b - 1, gate)
                        if n_ == 7 and b == 0:
                            nat_evac(nat_last, kn - 1)
                            for half_row in flush_m:
                                mod_row(half_row)
                            if diag_m is not None:
                                dve.wait_ge(mod_ok, flush_no(2 * diag_m + 1) + 1)
                                col = mod[:, diag_m * KD:(diag_m + 1) * KD].unsqueeze(2).broadcast_to([P, KD, P])
                                idb = ident[:, :].unsqueeze(1).broadcast_to([P, KD, P])
                                dve.tensor_tensor(gt_row[:, :].rearrange("p (k q) -> p k q", k=KD), idb, col,
                                                  ALU.mult).then_inc(gt_diag, 1)
                        if half == 1 and name in ADA:
                            ada(name, b, j)
                return lambda: add_out(ph, 3, gate)

            def rstd(n):
                dve.wait_ge(ss_ok, 4 * n + 4)
                link(dve.tensor_reduce(st[:, 0, :], ss4[:, :, :], AX.X, ALU.add))
                dve.tensor_scalar(st[:, 1, :], st[:, 0, :], 1.0 / D, EPS, ALU.mult, ALU.add).then_inc(rt_ok, 1)
                dve.wait_ge(rt_ok, 2 * n + 2)
                link(dve.reciprocal(st[:, 3, :], st[:, 2, :]))
                newton(st[:, 3, :], st[:, 1, :], st[:, 4, :], st[:, 5, :], st[:, 6, :])

            def newton(r, v, t0, t1, res):
                link(dve.tensor_tensor(t0, r, r, ALU.mult))
                link(dve.tensor_tensor(t1, t0, v, ALU.mult))
                link(dve.tensor_scalar(t1, t1, -0.5, 1.5, ALU.mult, ALU.add))
                link(dve.tensor_tensor(res, r, t1, ALU.mult))

            def turn_split(groups, count0):
                for g in groups:
                    dve.wait_ge(xt_f, count0 + g + 1)
                    src = buf_a[:, g % 2, :].rearrange("p (k t) -> p k t", k=2)
                    ks = slice(2 * g, 2 * g + 2)
                    dve.tensor_copy(act_hi[:, ks, :], src).then_inc(xt_hi, 1)
                    dve.wait_ge(xt_hi, count0 + g + 1)
                    dve.tensor_tensor(act_lo[:, ks, :], src, act_hi[:, ks, :].bitcast(F32), ALU.subtract)\
                        .then_inc(xt_lo, 1)

            def diagonals(n):
                rstd(n)
                for tt in range(TT):
                    dve.tensor_scalar(dg[:, tt, :], ident[:, :], st[:, 6, tt:tt + 1], None, ALU.mult)

            def gains(sc, g, k0, k1, ready):
                if (sc, k0) == (SC1, 0):
                    dve.wait_ge(mod_ok, 1)
                elif sc == SC1:
                    dve.wait_ge(mod_ok, 2)
                dve.scalar_tensor_tensor(out=gain[:, k0:k1], in0=mod[:, sc * KD + k0:sc * KD + k1], scalar=1.0,
                                         in1=par[:, PAR[g] + k0:PAR[g] + k1], op0=ALU.add, op1=ALU.mult)\
                    .then_inc(ready, 1)

            def norm(n, sh, sc, g, g0, n_):
                if n_ == 3:
                    diagonals(n)
                    dve.wait_ge(mod_ok, flush_no(2 * sc + 1) + 1)
                    gains(sc, g, 0, KD, diag_ok)
                norm_split(GROUPS_AT.get(n_, ()), n, sh, g0)

            def ffn(f, mid):
                for p, ng in enumerate(PARTS):
                    name = f"ffn{f}_in{p}"
                    ph = plan[name]
                    ffn_in(name, ng, mid)
                    oname = f"ffn{f}_out{p}"
                    tail = out_phase(oname, ng, ph.nat0 + ng - 1, lambda: hidden(ph, ng - 1),
                                    0 if f == 1 else 2,
                                    flush_m={"ffn1_out0": (4,), "ffn1_out1": (7,), "ffn1_out2": (10,),
                                             "ffn2_out0": (16,)}.get(oname, ()),
                                    diag_m={"ffn1_out0": GT1, "ffn2_out0": GT3}.get(oname))
                    nxt = {"ffn1_out0": 6, "ffn1_out1": 9}.get(oname)
                    mid = at_3(tail, nxt)
                return tail

            def at_3(tail, half_row):
                def run(n_):
                    if n_ == 3:
                        tail()
                        if half_row is not None:
                            mod_row(half_row)
                return run

            def angles():
                dve.wait_ge(rows_in, 64)
                link(dve.tensor_copy(st[:, 7, :], pos_i[:, :]))
                base = ang[:, 0, :, :]
                link(dve.tensor_tensor(base, st[:, 7, :].unsqueeze(2).broadcast_to([P, TT, HALF]),
                                       inv_f[:, :].unsqueeze(1).broadcast_to([P, TT, HALF]), ALU.mult))
                dve.tensor_scalar(ang[:, 2, :, :], base, 1.0 / (2 * np.pi), None, ALU.mult)
                link(dve.tensor_scalar(ang[:, 3, :, :], base, 1.0 / (2 * np.pi), 0.25, ALU.mult, ALU.add))
                link(dve.tensor_scalar(ang[:, 2:4, :, :], ang[:, 2:4, :, :], ROUND_MAGIC, None, ALU.add))
                link(dve.tensor_scalar(ang[:, 2:4, :, :], ang[:, 2:4, :, :], ROUND_MAGIC, None, ALU.subtract))
                for part in (TWO_PI_A, TWO_PI_B, TWO_PI_C):
                    src = (base, base) if part == TWO_PI_A else (ang[:, 4, :, :], ang[:, 5, :, :])
                    dve.scalar_tensor_tensor(out=ang[:, 4, :, :], in0=ang[:, 2, :, :], scalar=-part, in1=src[0],
                                             op0=ALU.mult, op1=ALU.add)
                    link(dve.scalar_tensor_tensor(out=ang[:, 5, :, :], in0=ang[:, 3, :, :], scalar=-part, in1=src[1],
                                                  op0=ALU.mult, op1=ALU.add))
                link(dve.tensor_scalar(ang[:, 5, :, :], ang[:, 5, :, :], float(np.pi / 2), None, ALU.add))
                dve.tensor_scalar(ang[:, 4:6, :, :], ang[:, 4:6, :, :], 3.1415925, -3.1415925, ALU.min, ALU.max)\
                    .then_inc(rope_ang, 1)

            for i in range(HALF):
                dve.memset(inv_f[:, i:i + 1], float(np.float32(ROPE_THETA ** (-i * 2.0 / ROT))))
            dve.wait_ge(par_tr, 1)
            dve.tensor_copy(par[:, 0:NPAR], px[:, 0, 0:NPAR]).then_inc(par_ok, 1)
            dve.tensor_copy(bada[:, :], px[:, 0, P:P + NB]).then_inc(bada_ok, 1)
            dve.wait_ge(par_ok, 1)
            dve.wait_ge(bada_ok, 1)
            dve.wait_ge(cond_ok, 1)
            angles()
            diagonals(0)
            over(dve, 4, lambda i, first: [ada("start0", i, j) for j in range(8)])

            def first_norm(n_):
                if n_ == 0:
                    mod_row(0)
                    gains(SC1, "g1", 0, KD // 2, diag_ok)
                turn_split(FIRST_AT.get(n_, ()) if n_ < 8 else (), 0)
                for tile in START1_TILES.get(n_, ()):
                    ada("start1", tile // 8, tile % 8)
                if n_ == 7:
                    mod_row(2)
                    gains(SC1, "g1", KD // 2, KD, gain_ok)
                turn_split(FIRST_AT.get(n_, ()) if n_ >= 8 else (), 0)
            tail = ffn(1, first_norm)

            def mid2(n_):
                if n_ == 3:
                    tail()
                    mod_row(11)
                norm(1, SH2, SC2, "g2", 8, n_)

            ph = plan["proj"]

            def rope():
                dve.wait_ge(trig_ok, 1)
                dve.wait_ge(pa_free, ph.a0 + 3)
                dve.wait_ge(pb_free, ph.b0 + 2)
                HR = HQ + KV
                for tt in range(TT):
                    qk = proj[:, tt, 0:OV].rearrange("p (h d) -> p h d", d=HD)
                    x1, x2 = qk[:, :, 0:HALF], qk[:, :, HALF:ROT]
                    sin = ang[:, 6, tt, :].unsqueeze(1).broadcast_to([P, HR, HALF])
                    cos = ang[:, 7, tt, :].unsqueeze(1).broadcast_to([P, HR, HALF])
                    r = [rope_t[:, k, :].rearrange("p (h d) -> p h d", d=HALF) for k in range(4)]
                    dve.tensor_tensor(r[0], x1, cos, ALU.mult)
                    dve.tensor_tensor(r[1], x2, sin, ALU.mult)
                    dve.tensor_tensor(r[2], x2, cos, ALU.mult)
                    link(dve.tensor_tensor(r[3], x1, sin, ALU.mult))
                    dve.tensor_tensor(x1, r[0], r[1], ALU.subtract)
                    link(dve.tensor_tensor(x2, r[2], r[3], ALU.add))
                dve.memset(xpad[:, :, 0:CONV - 1], 0.0).then_inc(rope_ok, 1)

            def conv(hd):
                dve.wait_ge(m_pad, hd + 1)
                dve.wait_ge(rope_ok, 1)
                for s in range(CONV):
                    for qk in (0, 1):
                        cw = PAR["conv_w"] + s * (MQK2 // P) + qk * MH + hd
                        src = xpad[:, qk, s:s + T].rearrange("p (t c) -> p t c", t=TT)
                        dst = m_cols(hd, qk)
                        if s == 0:
                            ins = dve.tensor_scalar(dst, src, par[:, cw:cw + 1], None, ALU.mult)
                        else:
                            ins = dve.scalar_tensor_tensor(out=dst, in0=src, scalar=par[:, cw:cw + 1],
                                                           in1=dst, op0=ALU.mult, op1=ALU.add)
                    if s < CONV - 1:
                        link(ins)
                ins.then_inc(m_conv, 1)

            def proj_body(i, first, step=None):
                for n_, (j, half, k0, n) in enumerate(units(8, 4)):
                    split(ph, i, j, half, n)
                    if first:
                        mid2(n_)
                    if half == 1:
                        ada("proj", i, j)
                    if step:
                        step(n_)

            def proj_step(n_):
                if n_ == 4:
                    rope()
                if n_ in (9, 11, 13, 15):
                    conv((n_ - 9) // 2)
            over(dve, 3, proj_body)
            proj_body(3, False, proj_step)

            rp = plan["rest"]
            for n_, (j, half, k0, n) in enumerate(units(4, 4)):
                split(rp, 0, j, half, n, REST_W)
                if n_ == 0:
                    dve.wait_ge(rows_in, 64)
                    dve.wait_ge(pa_free, rp.a0)
                    link(dve.tensor_tensor(m_st[:, 4:6, :], proj[:, :, OF:OF + MH],
                                           gb_row[:, 1, :].unsqueeze(1).broadcast_to([P, TT, MH]), ALU.add))
                    dve.tensor_scalar(m_st[:, 0:2, :], m_st[:, 4:6, :], 0.0, None, ALU.min)
                    link(dve.tensor_scalar(m_st[:, 6:8, :], m_st[:, 4:6, :], -1.0, None, ALU.mult))
                    dve.tensor_tensor(m_st[:, 8:10, :], m_st[:, 4:6, :], m_st[:, 6:8, :], ALU.max).then_inc(g_abs, 1)
                if n_ == 2:
                    mod_row(12)
                    dve.wait_ge(g_ln, 1)
                    dve.tensor_tensor(m_st[:, 0:2, :], m_st[:, 0:2, :], m_st[:, 8:10, :], ALU.subtract)\
                        .then_inc(g_logf, 1)
                if n_ == 6:
                    dve.wait_ge(g_cum, 1)
                    dve.tensor_copy(m_st[:, 2:4, :], pm[:, 0:2 * MH].rearrange("p (t a) -> p t a", t=TT))
                    link(dve.tensor_tensor(m_st[:, 6:8, :], proj[:, :, OI:OI + MH],
                                           gb_row[:, 0, :].unsqueeze(1).broadcast_to([P, TT, MH]), ALU.add))
                    link(dve.tensor_tensor(m_st[:, 4:6, :], m_st[:, 6:8, :], m_st[:, 2:4, :], ALU.subtract))
                    dve.wait_ge(flushed, flush_no(12) + 1)
                    for tt in range(TT):
                        ins = dve.tensor_tensor(dgm[:, tt, :, :], ident[:, :].unsqueeze(1).broadcast_to([P, MH, P]),
                                                m_st[:, 4 + tt, :].unsqueeze(2).broadcast_to([P, MH, P]), ALU.mult)
                    dve.tensor_copy(h_sq[:, 3, :, :], m_st[:, 2:4, :]).then_inc(g_diag, 1)

            heads_base = steps[0]
            count = [0]

            def chain(i, ins):
                count[0] += 1
                ins.then_inc(dve_step, 1)
                dve.wait_ge(dve_step, heads_base + i * HEAD_LINKS + count[0])

            def soft_a(i, n):
                dve.wait_ge(sc_mm, n + 1)
                own = mask[:, P:2 * P].unsqueeze(1).broadcast_to([P, 2, P])
                both = mask[:, :].unsqueeze(1).broadcast_to([P, 2, 2 * P])
                dve.scalar_tensor_tensor(out=s_sb[:, :, 0:P], in0=pm[:, 0:2 * P].rearrange("p (a t) -> p a t", a=2),
                                         scalar=HD ** -0.5, in1=own, op0=ALU.mult, op1=ALU.add)
                chain(i, dve.scalar_tensor_tensor(out=s_sb[:, :, P:3 * P],
                                                  in0=pr[:, :].rearrange("p (a t) -> p a t", a=2),
                                                  scalar=HD ** -0.5, in1=both, op0=ALU.mult, op1=ALU.add))
                dve.tensor_reduce(m_st[:, 2, 0:2], s_sb[:, :, 0:P], AX.X, ALU.max)
                chain(i, dve.tensor_reduce(m_st[:, 2, 2:4], s_sb[:, :, P:3 * P], AX.X, ALU.max))
                sink = sink_row[:, bass.ds(n * 2, 2)].unsqueeze(1).broadcast_to([P, 2, 2])
                mx = m_st[:, 3, :].rearrange("p (b a) -> p b a", b=2)
                chain(i, dve.tensor_tensor(mx, m_st[:, 2, :].rearrange("p (b a) -> p b a", b=2), sink, ALU.max))
                dve.tensor_tensor(m_st[:, 5, :].rearrange("p (b a) -> p b a", b=2), sink, mx, ALU.subtract)
                dve.tensor_scalar(m_st[:, 4, :], m_st[:, 3, :], -1.0, None, ALU.mult).then_inc(mx_ok, 1)

            def soft_b(i, n):
                dve.wait_ge(p_ok, n + 1)
                chain(i, dve.tensor_tensor(m_st[:, 7, :], m_st[:, 7, :], m_st[:, 6, :], ALU.add))
                chain(i, dve.reciprocal(m_st[:, 8, :], m_st[:, 7, :]))

            def att_out(n):
                dve.wait_ge(o_mm, n + 1)
                for b in range(TT):
                    dst = proj[:, b, bass.ds(n * (2 * HD), 2 * HD)].rearrange("p (a d) -> p a d", a=2)
                    src = pm[:, 2 * b * HD:2 * (b + 1) * HD].rearrange("p (a d) -> p a d", a=2)
                    ins = dve.tensor_tensor(dst, src, m_st[:, 8, 2 * b:2 * b + 2].unsqueeze(2).broadcast_to([P, 2, HD]),
                                            ALU.mult)
                ins.then_inc(o_ok, 1)

            def heads_step(i, n_):
                if n_ == 1:
                    rr = r_row[:, bass.ds(i, 1), :].rearrange("p a t -> p (a t)")
                    dve.wait_ge(g_rowok, 1)
                    if not (isinstance(i, int) and i == 0):
                        dve.wait_ge(m_ss, i)
                    dve.tensor_tensor(w_sb[:, 0:P], rr[:, 0:P], mask[:, P:2 * P], ALU.add)
                    dve.tensor_copy(w_sb[:, P:2 * P], rr[:, 0:P])
                    chain(i, dve.tensor_tensor(w_sb[:, 2 * P:3 * P], rr[:, P:T], mask[:, P:2 * P], ALU.add))
                    dve.tensor_reduce(m_st[:, 12, 2:3], w_sb[:, 0:P], AX.X, ALU.max)
                    chain(i, dve.tensor_reduce(m_st[:, 12, 3:4], w_sb[:, P:3 * P], AX.X, ALU.max))
                    chain(i, dve.tensor_scalar(m_st[:, 12, 0:2], m_st[:, 12, 2:4], -1.0, None, ALU.mult))
                    dve.tensor_tensor(m_st[:, 13, 2:4], m_st[:, 12, 0:2],
                                      h_sq[:, 3, :, bass.ds(i, 1)].rearrange("p t a -> p (t a)"), ALU.subtract)\
                        .then_inc(m_max, 1)
                if n_ == 4:
                    dve.wait_ge(m_sc, i + 1)
                    dve.wait_ge(m_w, i + 1)
                    dve.scalar_tensor_tensor(out=w_sb[:, 0:P], in0=px[:, 1, 0:P], scalar=DK ** -0.5,
                                             in1=w_sb[:, 0:P], op0=ALU.mult, op1=ALU.mult,
                                             accum_out=m_st[:, 10, 0:1])
                    dve.scalar_tensor_tensor(out=w_sb[:, P:3 * P], in0=px[:, 1, P:3 * P], scalar=DK ** -0.5,
                                             in1=w_sb[:, P:3 * P], op0=ALU.mult, op1=ALU.mult,
                                             accum_out=m_st[:, 10, 1:2]).then_inc(m_a, 1)
                if n_ == 5:
                    soft_a(i, 2 * i)
                if n_ == 6:
                    dve.wait_ge(m_a, i + 1)
                    chain(i, dve.tensor_scalar(m_st[:, 11, 0:2], m_st[:, 10, 0:2], -1.0, None, ALU.mult))
                    chain(i, dve.tensor_tensor(m_st[:, 11, 0:2], m_st[:, 10, 0:2], m_st[:, 11, 0:2], ALU.max))
                    chain(i, dve.tensor_tensor(m_st[:, 11, 0:2], m_st[:, 11, 0:2], m_st[:, 13, 0:2], ALU.max))
                    chain(i, dve.reciprocal(m_st[:, 11, 2:4], m_st[:, 11, 0:2]))
                if n_ == 8:
                    soft_b(i, 2 * i)
                if n_ == 10:
                    att_out(2 * i)
                if n_ == 11:
                    dve.wait_ge(m_num, i + 1)
                    for tt in range(TT):
                        ins = dve.tensor_scalar(proj[:, tt, bass.ds(i * MV + OMV, MV)], pr[:, tt * MV:(tt + 1) * MV],
                                                m_st[:, 11, 2 + tt:3 + tt], None, ALU.mult)
                    ins.then_inc(m_h, 1)
                if n_ == 13:
                    dve.wait_ge(m_ss, i + 1)
                    soft_a(i, 2 * i + 1)
                if n_ == 15:
                    soft_b(i, 2 * i + 1)
                    att_out(2 * i + 1)
            gp = plan["gates"]
            HEAD_LINKS = 17

            def gates_body(i, first):
                count[0] = 0
                for n_, (j, half, k0, n) in enumerate(units(8, 4)):
                    split(gp, i, j, half, n)
                    heads_step(i, n_)
                assert count[0] == HEAD_LINKS, count[0]
            over(dve, 4, gates_body)
            steps[0] = heads_base + 4 * HEAD_LINKS

            def head_norms():
                dve.wait_ge(m_ss, MH)
                dve.tensor_scalar(h_sq[:, 1, :, :], h_sq[:, 0, :, :], 1.0 / MV, EPS, ALU.mult, ALU.add)\
                    .then_inc(m_var, 1)
                dve.wait_ge(m_rt, 1)
                dve.wait_ge(m_var, 1)
                v, y = h_sq[:, 1, :, :], h_sq[:, 2, :, :]
                t0, t1, res = (m_st[:, k:k + 2, :] for k in (0, 2, 4))
                link(dve.reciprocal(res, y))
                newton(res, v, t0, t1, h_sq[:, 3, :, :])

            def head_gates():
                dve.wait_ge(proj_ok, 1)
                for hd in range(MH):
                    for tt in range(TT):
                        vs = slice(OMV + hd * MV, OMV + (hd + 1) * MV)
                        os = slice(OO + hd * MV, OO + (hd + 1) * MV)
                        ins = dve.scalar_tensor_tensor(out=proj[:, tt, vs], in0=proj[:, tt, vs],
                                                       scalar=h_sq[:, 3, tt, hd:hd + 1], in1=proj[:, tt, os],
                                                       op0=ALU.mult, op1=ALU.mult)
                    ins.then_inc(m_out, 1)

            ph = plan["up"]

            def mix_a(i):
                dve.wait_ge(unit_used, 2 * (ph.c0 + ph.per * i) + 4)
                dve.wait_ge(gate_sig, 2 * i + 1)
                dve.wait_ge(xt_lo, 24)
                dve.tensor_tensor(buf_a[:, :, :], pa[:, :, :], gates[:, :, bass.ds(i * NC, NC)], ALU.mult)\
                    .then_inc(pa_free, 1)

            def mix_b(i):
                dve.wait_ge(unit_used, 2 * (ph.c0 + ph.per * i) + 8)
                dve.wait_ge(gate_sig, 2 * i + 2)
                dve.tensor_tensor(buf_b[:, :, :], pb[:, :, :], gates[:, :, bass.ds(i * NC + D, NC)], ALU.mult)\
                    .then_inc(pb_free, 1)
                dve.wait_ge(pb_free, ph.b0 + i + 1)
                dve.wait_ge(pa_free, ph.a0 + i + 1)
                dve.tensor_tensor(buf_b[:, :, :], buf_b[:, :, :], buf_a[:, :, :], ALU.add).then_inc(nat_ok, 1)

            def up(i, first):
                for n_, (j, half, k0, n) in enumerate(units(4, 4)):
                    split(ph, i, j, half, n)
                    if n_ == 3:
                        if not first:
                            mix_b(i - 1)
                    if first and n_ == 2:
                        head_norms()
                    if first:
                        turn_split(OUT_AT.get(n_, ()), 16)
                    if first and n_ == 3:
                        head_gates()
                    if half == 1 and not first:
                        ada("up", i, j)
                    if first and n_ >= 4:
                        ada("up", i, n_ - 4)
                mix_a(i)
                if not first:
                    nat_evac(ph.nat0 + i - 1, i - 1)
            over(dve, 4, up)
            tail2 = out_phase("wout", 4, ph.nat0 + 3, lambda: mix_b(3), 1, flush_m=(14,), diag_m=GT2)

            def mid3(n_):
                if n_ == 3:
                    tail2()
                    mod_row(15)
                norm(2, SH3, SC3, "g3", 24, n_)
            ffn(2, mid3)()
            rstd(3)
            dve.wait_ge(fin_in, 16)
            for q in range(4):
                cols = slice((q % 2) * (D // 2), (q % 2 + 1) * (D // 2))
                dve.scalar_tensor_tensor(out=h[:, q // 2, cols], in0=h[:, q // 2, cols],
                                         scalar=st[:, 6, q // 2:q // 2 + 1], in1=fin_row[:, cols],
                                         op0=ALU.mult, op1=ALU.mult).then_inc(fin_ok, 1)


_INS = ['x', 'c', 'positions', 'w_ada', 'b_ada', 'norm1_g', 'ffn1_w_in', 'ffn1_w_out', 'norm2_g', 'w_in',
        'conv_w', 'conv_b', 'b_igate', 'b_fgate', 'sinks', 'mlstm_norm_g', 'w_att_up', 'w_mlstm_up',
        'w_out', 'norm3_g', 'ffn2_w_in', 'ffn2_w_out', 'final_g']


def kernel(**inputs):
    import numpy as _np
    import concourse.bacc as _bacc
    from concourse import mybir as _mybir
    from concourse.bass_utils import run_bass_kernel_spmd as _run

    nc = _bacc.Bacc("TRN2", target_bir_lowering=False, num_devices=1)
    arrays, args = {}, []
    for name in _INS:
        a = _np.ascontiguousarray(inputs[name])
        arrays[f"in_{name}_dram"] = a
        args.append(nc.dram_tensor(f"in_{name}_dram", a.shape, _mybir.dt.from_np(a.dtype), kind="ExternalInput").ap())
    shape = inputs["x"].shape
    args.append(nc.dram_tensor("out_0_dram", shape, _mybir.dt.float32, kind="ExternalOutput").ap())
    build(nc, *args)
    r = _run(nc, [arrays], core_ids=[0])
    return r.results[0]["out_0_dram"]
```
